# Optimizing a Trainium2 kernel written in Bass

```python
import numpy as np
import jax
import jax.numpy as jnp
from jax import lax

D_MODEL = 1024
BATCH = 1
SEQ = 2048
DEPTH = 4

CHUNK = 64
N_MIXERS = 4
N_RG = (DEPTH + 3) // 4
N_DN = (DEPTH + 2) // 4
N_POOL = (DEPTH + 1) // 4
N_SWA = DEPTH // 4
EPS = 1e-6
CONV_WIDTH = 4

RG_WIDTH = D_MODEL
RG_BLOCKS = 8
RG_BW = RG_WIDTH // RG_BLOCKS
RG_C = 8.0

DN_HEADS = 8
DN_DK = 128
DN_DV = 128
DN_QK = DN_HEADS * DN_DK
DN_V = DN_HEADS * DN_DV
DN_CONV_DIM = 2 * DN_QK + DN_V
DN_IN = DN_CONV_DIM + DN_V + 2 * DN_HEADS

POOL_WIDTH = D_MODEL
POOL_WINDOWS = (2, 4, 8, 16)
POOL_GROUPS = len(POOL_WINDOWS)
POOL_GW = POOL_WIDTH // POOL_GROUPS

SWA_HQ = 16
SWA_HKV = 2
SWA_GROUP = SWA_HQ // SWA_HKV
SWA_HD = 64
SWA_WINDOW = 128
SWA_KEY_CHUNKS = SWA_WINDOW // CHUNK
SWA_KLEN = SWA_KEY_CHUNKS * CHUNK
SWA_QD = SWA_HQ * SWA_HD
SWA_KD = SWA_HKV * SWA_HD
SWA_IN = 2 * SWA_QD + 2 * SWA_KD

N_BUCKETS = 32
MAX_DISTANCE = 128
NEG_INF = -1e30

kernel_name = 'hybrid_streaming_encoder'

def rms_norm(x, w):
    xf = x.astype(jnp.float32)
    y = xf * lax.rsqrt(jnp.mean(xf * xf, axis=-1, keepdims=True) + EPS)
    return (y * w.astype(jnp.float32)).astype(x.dtype)

def causal_dwconv(x, w):
    K, C = w.shape
    xp = jnp.pad(x, ((0, 0), (K - 1, 0), (0, 0)))
    return lax.conv_general_dilated(xp, w[:, None, :], window_strides=(1,), padding='VALID',
                                    dimension_numbers=('NWC', 'WIO', 'NWC'), feature_group_count=C)

def linear_scan(a, b):
    def combine(left, right):
        al, bl = left
        ar, br = right
        return al * ar, ar * bl + br
    _, hs = lax.associative_scan(combine, (a, b), axis=1)
    return hs

def rglru_mixer(h, w_in, conv_w, conv_b, gate_w, gate_b, lam, w_out):
    B, S, _ = h.shape
    u, gate = jnp.split(h @ w_in, 2, axis=-1)
    u = causal_dwconv(u, conv_w) + conv_b
    ub = u.reshape(B, S, RG_BLOCKS, RG_BW)
    gl = jnp.einsum('bsnk,nkgj->bsgnj', ub, gate_w).reshape(B, S, 2, RG_WIDTH) + gate_b
    gl = gl.astype(jnp.float32)
    r = jax.nn.sigmoid(gl[:, :, 0])
    i = jax.nn.sigmoid(gl[:, :, 1])
    log_a = -RG_C * r * jax.nn.softplus(-lam.astype(jnp.float32))
    a = jnp.exp(log_a)
    mult = jnp.sqrt(-jnp.expm1(2.0 * log_a))
    hs = linear_scan(a, mult * i * u.astype(jnp.float32))
    y = hs.astype(h.dtype) * jax.nn.silu(gate)
    return y @ w_out

def l2norm(t):
    return t * lax.rsqrt(jnp.sum(t * t, axis=-1, keepdims=True) + EPS)

def chunk_gated_delta(q, k, v, g, beta):
    B, S, H, DK = q.shape
    DV = v.shape[-1]
    C = CHUNK
    N = S // C
    q = q * (DK ** -0.5)

    def to_chunks(t):
        return t.reshape((B, N, C, H) + t.shape[3:]).swapaxes(2, 3)

    q, k, v, g, beta = (to_chunks(t) for t in (q, k, v, g, beta))
    g = jnp.cumsum(g, axis=-1)
    lower = np.tril(np.ones((C, C), dtype=bool))
    strict = np.tril(np.ones((C, C), dtype=bool), -1)
    diff = g[..., :, None] - g[..., None, :]
    decay = jnp.where(lower, jnp.exp(jnp.where(lower, diff, 0.0)), 0.0)
    kb = k * beta[..., None]
    A = jnp.where(strict, jnp.einsum('bnhik,bnhjk->bnhij', kb, k) * decay, 0.0)
    T = A + jnp.eye(C, dtype=jnp.float32)
    rhs = jnp.concatenate([v * beta[..., None], kb * jnp.exp(g)[..., None]], axis=-1)
    sol = lax.linalg.triangular_solve(T, rhs, left_side=True, lower=True, unit_diagonal=True)
    u_c, w_c = sol[..., :DV], sol[..., DV:]
    attn_intra = jnp.where(lower, jnp.einsum('bnhik,bnhjk->bnhij', q, k) * decay, 0.0)

    def step(state, xs):
        qc, kc, uc, wc, gc, ac = xs
        v_new = uc - jnp.einsum('bhck,bhkv->bhcv', wc, state)
        o = jnp.einsum('bhck,bhkv->bhcv', qc * jnp.exp(gc)[..., None], state) + \
            jnp.einsum('bhij,bhjv->bhiv', ac, v_new)
        g_last = gc[..., -1]
        k_dec = kc * jnp.exp(g_last[..., None] - gc)[..., None]
        state = state * jnp.exp(g_last)[..., None, None] + jnp.einsum('bhck,bhcv->bhkv', k_dec, v_new)
        return state, o

    xs = tuple(t.swapaxes(0, 1) for t in (q, k, u_c, w_c, g, attn_intra))
    state0 = jnp.zeros((B, H, DK, DV), jnp.float32)
    _, o = lax.scan(step, state0, xs)
    return o.transpose(1, 0, 3, 2, 4).reshape(B, S, H, DV)

def gdn_mixer(h, w_in, conv_w, a_log, dt_bias, norm_w, w_out):
    B, S, _ = h.shape
    proj = h @ w_in
    qkv = jax.nn.silu(causal_dwconv(proj[..., :DN_CONV_DIM], conv_w))
    z = proj[..., DN_CONV_DIM:DN_CONV_DIM + DN_V].reshape(B, S, DN_HEADS, DN_DV)
    beta_raw = proj[..., DN_CONV_DIM + DN_V:DN_CONV_DIM + DN_V + DN_HEADS]
    alpha_raw = proj[..., DN_CONV_DIM + DN_V + DN_HEADS:]
    qkv = qkv.astype(jnp.float32)
    q = l2norm(qkv[..., :DN_QK].reshape(B, S, DN_HEADS, DN_DK))
    k = l2norm(qkv[..., DN_QK:2 * DN_QK].reshape(B, S, DN_HEADS, DN_DK))
    v = qkv[..., 2 * DN_QK:].reshape(B, S, DN_HEADS, DN_DV)
    beta = jax.nn.sigmoid(beta_raw.astype(jnp.float32))
    g = -jnp.exp(a_log.astype(jnp.float32)) * jax.nn.softplus(
        alpha_raw.astype(jnp.float32) + dt_bias.astype(jnp.float32))
    o = chunk_gated_delta(q, k, v, g, beta)
    o = rms_norm(o, norm_w).astype(h.dtype) * jax.nn.silu(z)
    return o.reshape(B, S, DN_V) @ w_out

def pool_mixer(h, w_in, group_w, group_b, scale, w_out):
    B, S, _ = h.shape
    u, gate = jnp.split(h @ w_in, 2, axis=-1)
    uf = u.astype(jnp.float32)
    cs = jnp.cumsum(uf, axis=1)
    cs0 = jnp.pad(cs, ((0, 0), (1, 0), (0, 0)))
    count = jnp.arange(1, S + 1, dtype=jnp.float32)[None, :, None]
    outs = []
    for gi, win in enumerate(POOL_WINDOWS):
        sl = slice(gi * POOL_GW, (gi + 1) * POOL_GW)
        lag = jnp.pad(cs0[:, :S - win + 1, sl], ((0, 0), (win - 1, 0), (0, 0)))
        mean = (cs[:, :, sl] - lag) / jnp.minimum(count, float(win))
        outs.append(mean - uf[:, :, sl])
    p = jnp.stack(outs, axis=2).astype(h.dtype)
    p = jnp.einsum('bsgi,gio->bsgo', p, group_w).reshape(B, S, POOL_WIDTH) + group_b
    y = (p * scale) * jax.nn.silu(gate)
    return y @ w_out

def t5_buckets(rel):
    nb = N_BUCKETS // 2
    ret = (rel > 0).astype(np.int32) * nb
    n = np.abs(rel)
    max_exact = nb // 2
    large = max_exact + (np.log(np.maximum(n, 1) / max_exact) / np.log(MAX_DISTANCE / max_exact)
                         * (nb - max_exact)).astype(np.int32)
    large = np.minimum(large, nb - 1)
    return ret + np.where(n < max_exact, n, large)

def swa_mixer(h, w_in, b_in, sinks, rel_bias, w_out):
    B, S, _ = h.shape
    N = S // CHUNK
    pad = SWA_KLEN - CHUNK
    proj = h @ w_in + b_in
    q = proj[..., :SWA_QD].reshape(B, N, CHUNK, SWA_HKV, SWA_GROUP, SWA_HD)
    k = proj[..., SWA_QD:SWA_QD + SWA_KD].reshape(B, S, SWA_HKV, SWA_HD)
    v = proj[..., SWA_QD + SWA_KD:SWA_QD + 2 * SWA_KD].reshape(B, S, SWA_HKV, SWA_HD)
    gate = proj[..., SWA_QD + 2 * SWA_KD:]
    kp = jnp.pad(k, ((0, 0), (pad, 0), (0, 0), (0, 0)))
    vp = jnp.pad(v, ((0, 0), (pad, 0), (0, 0), (0, 0)))
    kb = jnp.concatenate([kp[:, j * CHUNK:j * CHUNK + S].reshape(B, N, CHUNK, SWA_HKV, SWA_HD)
                          for j in range(SWA_KEY_CHUNKS)], axis=2)
    vb = jnp.concatenate([vp[:, j * CHUNK:j * CHUNK + S].reshape(B, N, CHUNK, SWA_HKV, SWA_HD)
                          for j in range(SWA_KEY_CHUNKS)], axis=2)
    logits = jnp.einsum('bnqhgd,bnkhd->bnhgqk', q, kb).astype(jnp.float32) * (SWA_HD ** -0.5)
    rel = np.arange(SWA_KLEN)[None, :] - pad - np.arange(CHUNK)[:, None]
    bias = rel_bias[t5_buckets(rel)].astype(jnp.float32)
    bias = jnp.transpose(bias, (2, 0, 1)).reshape(SWA_HKV, SWA_GROUP, CHUNK, SWA_KLEN)
    kabs = np.arange(N)[:, None] * CHUNK - pad + np.arange(SWA_KLEN)[None, :]
    valid = (kabs >= 0)[None, :, None, None, None, :]
    logits = jnp.where(valid, logits + bias, NEG_INF)
    sink = sinks.astype(jnp.float32).reshape(SWA_HKV, SWA_GROUP)[:, :, None, None]
    m = jnp.maximum(jnp.max(logits, axis=-1, keepdims=True), sink)
    e = jnp.exp(logits - m)
    p = e / (jnp.sum(e, axis=-1, keepdims=True) + jnp.exp(sink - m))
    out = jnp.einsum('bnhgqk,bnkhd->bnqhgd', p.astype(h.dtype), vb).reshape(B, S, SWA_QD)
    y = out * jax.nn.silu(gate)
    return y @ w_out

def setup_inputs(seed: int = 0) -> dict:
    key = jax.random.key(seed)
    ks = iter(jax.random.split(key, 40))

    def nrm(shape, s):
        return s * jax.random.normal(next(ks), shape, jnp.float32)

    x = nrm((BATCH, SEQ, D_MODEL), 1.0)
    c = nrm((BATCH, D_MODEL), 1.0)
    ada_w = nrm((DEPTH, D_MODEL, 3 * D_MODEL), 0.5 * D_MODEL ** -0.5)
    ada_b = nrm((DEPTH, 3 * D_MODEL), 0.02)
    norm_w = 1.0 + nrm((DEPTH, D_MODEL), 0.02)
    rel_bias = nrm((N_BUCKETS, SWA_HQ), 0.5)
    final_norm_w = 1.0 + nrm((D_MODEL,), 0.02)

    rg_w_in = nrm((N_RG, D_MODEL, 2 * RG_WIDTH), D_MODEL ** -0.5)
    rg_conv_w = nrm((N_RG, CONV_WIDTH, RG_WIDTH), CONV_WIDTH ** -0.5)
    rg_conv_b = nrm((N_RG, RG_WIDTH), 0.02)
    rg_gate_w = nrm((N_RG, RG_BLOCKS, RG_BW, 2, RG_BW), RG_BW ** -0.5)
    rg_gate_b = nrm((N_RG, 2, RG_WIDTH), 0.02)
    a_c = jax.random.uniform(next(ks), (N_RG, RG_WIDTH), jnp.float32, minval=0.9, maxval=0.999)
    s = a_c ** (1.0 / RG_C)
    rg_lambda = jnp.log(s) - jnp.log1p(-s)
    rg_w_out = nrm((N_RG, RG_WIDTH, D_MODEL), RG_WIDTH ** -0.5)

    dn_w_in = nrm((N_DN, D_MODEL, DN_IN), D_MODEL ** -0.5)
    dn_conv_w = nrm((N_DN, CONV_WIDTH, DN_CONV_DIM), CONV_WIDTH ** -0.5)
    dn_a_log = jnp.log(jax.random.uniform(next(ks), (N_DN, DN_HEADS), jnp.float32, minval=1.0, maxval=16.0))
    dt = jnp.exp(jax.random.uniform(next(ks), (N_DN, DN_HEADS), jnp.float32,
                                    minval=float(np.log(1e-3)), maxval=float(np.log(1e-1))))
    dn_dt_bias = dt + jnp.log(-jnp.expm1(-dt))
    dn_norm_w = 1.0 + nrm((N_DN, DN_DV), 0.02)
    dn_w_out = nrm((N_DN, DN_V, D_MODEL), DN_V ** -0.5)

    pool_w_in = nrm((N_POOL, D_MODEL, 2 * POOL_WIDTH), D_MODEL ** -0.5)
    pool_group_w = nrm((N_POOL, POOL_GROUPS, POOL_GW, POOL_GW), POOL_GW ** -0.5)
    pool_group_b = nrm((N_POOL, POOL_WIDTH), 0.02)
    pool_scale = 1.0 + nrm((N_POOL, POOL_WIDTH), 0.1)
    pool_w_out = nrm((N_POOL, POOL_WIDTH, D_MODEL), POOL_WIDTH ** -0.5)

    swa_w_in = nrm((N_SWA, D_MODEL, SWA_IN), D_MODEL ** -0.5)
    swa_b_in = nrm((N_SWA, SWA_IN), 0.02)
    swa_sinks = nrm((N_SWA, SWA_HQ), 0.5)
    swa_w_out = nrm((N_SWA, SWA_QD, D_MODEL), SWA_QD ** -0.5)

    return {'x': x, 'c': c, 'ada_w': ada_w, 'ada_b': ada_b, 'norm_w': norm_w,
            'rel_bias': rel_bias, 'final_norm_w': final_norm_w,
            'rg_w_in': rg_w_in, 'rg_conv_w': rg_conv_w, 'rg_conv_b': rg_conv_b,
            'rg_gate_w': rg_gate_w, 'rg_gate_b': rg_gate_b, 'rg_lambda': rg_lambda, 'rg_w_out': rg_w_out,
            'dn_w_in': dn_w_in, 'dn_conv_w': dn_conv_w, 'dn_a_log': dn_a_log, 'dn_dt_bias': dn_dt_bias,
            'dn_norm_w': dn_norm_w, 'dn_w_out': dn_w_out,
            'pool_w_in': pool_w_in, 'pool_group_w': pool_group_w, 'pool_group_b': pool_group_b,
            'pool_scale': pool_scale, 'pool_w_out': pool_w_out,
            'swa_w_in': swa_w_in, 'swa_b_in': swa_b_in, 'swa_sinks': swa_sinks, 'swa_w_out': swa_w_out}

def reference(x, c, ada_w, ada_b, norm_w, rel_bias, final_norm_w,
              rg_w_in, rg_conv_w, rg_conv_b, rg_gate_w, rg_gate_b, rg_lambda, rg_w_out,
              dn_w_in, dn_conv_w, dn_a_log, dn_dt_bias, dn_norm_w, dn_w_out,
              pool_w_in, pool_group_w, pool_group_b, pool_scale, pool_w_out,
              swa_w_in, swa_b_in, swa_sinks, swa_w_out):
    cond = jax.nn.silu(c)
    for layer in range(DEPTH):
        kind, j = layer % N_MIXERS, layer // N_MIXERS
        mod = cond @ ada_w[layer] + ada_b[layer]
        shift, scale, gate = jnp.split(mod[:, None, :], 3, axis=-1)
        h = rms_norm(x, norm_w[layer]) * (1.0 + scale) + shift
        if kind == 0:
            y = rglru_mixer(h, rg_w_in[j], rg_conv_w[j], rg_conv_b[j], rg_gate_w[j], rg_gate_b[j],
                            rg_lambda[j], rg_w_out[j])
        elif kind == 1:
            y = gdn_mixer(h, dn_w_in[j], dn_conv_w[j], dn_a_log[j], dn_dt_bias[j], dn_norm_w[j], dn_w_out[j])
        elif kind == 2:
            y = pool_mixer(h, pool_w_in[j], pool_group_w[j], pool_group_b[j], pool_scale[j], pool_w_out[j])
        else:
            y = swa_mixer(h, swa_w_in[j], swa_b_in[j], swa_sinks[j], rel_bias, swa_w_out[j])
        x = x + gate * y
    return rms_norm(x, final_norm_w)


_drawn_inputs = setup_inputs


def setup_inputs(seed=0):
    import zlib

    import numpy as np

    out = dict(_drawn_inputs(seed))
    spreads = {}
    factors = {'norm_w': 5.152,
     'rel_bias': 4.221,
     'final_norm_w': 2.745,
     'rg_gate_b': 8.0,
     'dn_norm_w': 8.0,
     'pool_group_b': 8.0,
     'pool_scale': 3.646,
     'swa_b_in': 8.0,
     'swa_sinks': 8.0}
    for name, (base, spread) in spreads.items():
        noise = np.random.default_rng([zlib.crc32(name.encode()), seed]).standard_normal(out[name].shape)
        drawn = base * np.exp(spread * noise) if base else spread * noise
        out[name] = jnp.asarray(drawn.astype(out[name].dtype))
    for name, factor in factors.items():
        out[name] = (out[name] * factor).astype(out[name].dtype)
    return out
```

```python
import concourse.bass as bass
from concourse import mybir
from contextlib import ExitStack

F32 = mybir.dt.float32
F32R = mybir.dt.float32r
ACT = mybir.ActivationFunctionType
ALU = mybir.AluOpType
AX_X = mybir.AxisListType.X

P = 128
D = 1024
KT = D // P
CH = 512
HALF = 1024
NCH = HALF // CH
EPS = 1e-6
SEMS_A_PHASE = 76
ADA_BUFS = 4


def each(eng, n, body):
    if n > 1:
        with eng.Fori(0, n - 1) as i:
            body(i, False)
    body(n - 1, True)


class Steps:

    def __init__(self, eng, sem, base=0):
        self.eng, self.sem, self.base, self.n = eng, sem, base, 0

    def done(self, ins):
        self.n += 1
        ins.then_inc(self.sem, 1)
        self.eng.wait_ge(self.sem, self.base + self.n)


class Core:

    def __init__(self, nc, ctx):
        self.nc, self.ctx = nc, ctx
        self.phase_sems, self.phase_n, self.h_n = [], 0, 0
        self.bank = [ctx.enter_context(nc.psum_tensor(f"bank{i}", [P, CH], F32)) for i in range(8)]

    def sb(self, name, shape, dt=F32, ctx=None):
        return (ctx or self.ctx).enter_context(self.nc.sbuf_tensor(name, shape, dt))

    def begin_phase(self):
        for handle in self.phase_sems:
            self.nc.release_semaphore(handle)
        self.phase_sems, self.phase_n = [], self.phase_n + 1

    def _range(self, n):
        first = 100 + SEMS_A_PHASE * (n % 2)
        return range(first, first + SEMS_A_PHASE)

    def open_h(self):
        self.h_ctx = ExitStack()
        self.h_n += 1
        self.h_hi = self.sb(f"h_hi{self.h_n}", [P, KT, HALF], F32R, self.h_ctx)
        self.h_lo = self.sb(f"h_lo{self.h_n}", [P, KT, HALF], F32R, self.h_ctx)

    def close_h(self):
        self.h_ctx.close()

    def sem(self, name):
        num = self._range(self.phase_n)[len(self.phase_sems)]
        self.phase_sems.append(self.nc.alloc_semaphore(name, num=num))
        return self.phase_sems[-1]

    def clear_last_phase(self, sp):
        if self.phase_n > 1:
            sp.sem_clear(self._range(self.phase_n - 1))


class Weights:

    def __init__(self, core, ctx, tag, slots):
        self.nc, self.slots = core.nc, slots
        self.raw = [core.sb(f"{tag}_w_raw{i}", [P, KT, P], F32, ctx) for i in range(2)]
        self.hi = [core.sb(f"{tag}_w_hi{i}", [P, KT, P], F32R, ctx) for i in range(slots)]
        self.lo = [core.sb(f"{tag}_w_lo{i}", [P, KT, P], F32R, ctx) for i in range(slots)]
        self.arrived = [core.sem(f"{tag}_w_arrived{i}") for i in range(2)]
        self.rounded = core.sem(f"{tag}_w_rounded")
        self.split = core.sem(f"{tag}_w_split")
        self.projected = core.sem(f"{tag}_projected")

    def open(self, pe, pool, credit):
        self.credit = credit
        pe.sem_inc(self.projected, credit)
        pool.sem_inc(self.split, 2)

    def load(self, sp, src, j, first=0):
        sp.wait_ge(self.split, first + j + 1)
        sp.dma_start(self.raw[j % 2][:, :, :], src).then_inc(self.arrived[j % 2], 16)

    def round(self, act, j, free, first=0, arrivals=0):
        act.wait_ge(self.arrived[j % 2], arrivals + 16 * (j // 2) + 16)
        act.wait_ge(self.projected, free)
        self.nc.scalar.activation(self.hi[j % self.slots][:, :, :], self.raw[j % 2][:, :, :],
                                  ACT.Copy).then_inc(self.rounded, 1)

    def subtract(self, pool, j, first=0):
        pool.wait_ge(self.rounded, first + j + 1)
        self.nc.gpsimd.tensor_tensor(self.lo[j % self.slots][:, :, :], self.raw[j % 2][:, :, :],
                                     self.hi[j % self.slots][:, :, :].bitcast(F32),
                                     ALU.subtract).then_inc(self.split, 1)

    def multiply(self, pe, out, j, x_hi, x_lo, cols, first=0, waits=(), each_k=None):
        slot = j % self.slots
        pe.wait_ge(self.split, first + j + 3)
        for k in range(KT):
            if each_k:
                pe.wait_ge(*each_k[k])
            for n, (w, x) in enumerate(((self.hi, x_hi), (self.hi, x_lo), (self.lo, x_hi))):
                if k == KT - 1 and n == 2:
                    for sem, value in waits:
                        pe.wait_ge(sem, value)
                ins = self.nc.tensor.matmul(out, w[slot][:, k, :], x[:, k, cols],
                                            start=(k == 0 and n == 0), stop=(k == KT - 1 and n == 2))
        ins.then_inc(self.projected, 1)


def wtile(w, col):
    return w.rearrange("(t p) n -> p t n", p=P)[:, :, col]


def stack_rows(parts):
    rows, at = {}, 0
    for name, n in parts:
        rows[name] = at
        at += n
    assert at <= P, parts
    return rows


def setup_phase(core, A, depth):
    core.begin_phase()
    nc = core.nc
    core.ident = core.sb("ident", [P, P])
    core.ones = core.sb("ones", [P, P])
    core.eps = core.sb("eps", [P, 1])
    core.modA = core.sb("mod_scale", [P, depth * KT])
    core.modB = core.sb("mod_shift", [P, depth * KT])
    core.modG = core.sb("mod_gate", [P, depth * KT])
    core.final_w = core.sb("final_w", [P, KT])
    parts1 = [("c", 8), ("final", 8), ("rg_conv_w", 32), ("rg_conv_b", 8), ("rg_gate_b", 16), ("rg_lambda", 8)]
    if depth > 2:
        parts1 += [("pool_b", 8), ("pool_scale", 8)]
    if depth > 3:
        parts1 += [("swa_b", 18)]
    if depth > 1:
        parts1 += [("dn_norm", 1)]
    r1 = core.r1 = stack_rows(parts1)
    core.col1 = core.sb("vectors1", [P, P])
    core.rg_par = core.sb("rg_par", [P, KT, 13])
    n_stacks = 2
    if depth > 1:
        core.dn_par = core.sb("dn_conv_w", [P, P])
        n_stacks = 3
    with ExitStack() as ctx:
        row = [core.sb(f"stack{i}", [P, P], F32, ctx) for i in range(n_stacks)]
        col0 = core.sb("vectors0", [P, P], F32, ctx)
        cond = core.sb("cond", [P, KT], F32, ctx)
        cond_t = core.sb("cond_t", [P, KT], F32, ctx)
        mod = core.sb("mod", [P, depth * 24], F32, ctx)
        lam = core.sb("lam", [P, 4, KT], F32, ctx)
        ada = [core.sb(f"ada{i}", [P, 3 * D], F32, ctx) for i in range(ADA_BUFS)]
        acc = core.sb("ada_sums", [P, 3 * D], F32, ctx)
        s_row = core.sem("stacks_loaded")
        s_zero = core.sem("stacks_zeroed")
        s_const = core.sem("constants_made")
        s_tr = core.sem("stacks_transposed")
        s_col = core.sem("columns_ready")
        s_tanh = core.sem("setup_act")
        s_cond = core.sem("cond_ready")
        s_ada = [core.sem(f"ada_loaded{i}") for i in range(ADA_BUFS)]
        s_used = core.sem("ada_used")
        s_acc = core.sem("ada_sums_reduced")
        s_mod = core.sem("mod_ready")
        s_dve = core.sem("setup_dve")
        loads = [(1, "c", A["c"], 8), (1, "final", A["final_norm_w"].rearrange("(a n) -> a n", a=1), 8),
                 (1, "rg_conv_w", A["rg_conv_w"][0], 32), (1, "rg_conv_b", A["rg_conv_b"], 8),
                 (1, "rg_gate_b", A["rg_gate_b"][0], 16), (1, "rg_lambda", A["rg_lambda"], 8)]
        if depth > 2:
            loads += [(1, "pool_b", A["pool_group_b"], 8), (1, "pool_scale", A["pool_scale"], 8)]
        if depth > 3:
            loads += [(1, "swa_b", A["swa_b_in"], 18)]
        if depth > 1:
            loads += [(1, "dn_norm", A["dn_norm_w"], 1)]
        loads += [(0, 0, A["ada_b"], depth * 24), (0, depth * 24, A["norm_w"], depth * 8)]
        if depth > 1:
            loads += [(2, 0, A["dn_conv_w"][0], 96)]
        with nc.Block() as block:
            @block.sync
            def _(sp):
                core.clear_last_phase(sp)
                sp.wait_ge(s_zero, n_stacks)
                for i, at, src, n in loads:
                    at = r1[at] if isinstance(at, str) else at
                    view = src.rearrange("a (b p) -> (a b) p", p=P)
                    sp.dma_start(row[i][at:at + n, :], view).then_inc(s_row, 16)
                with sp.Fori(0, depth) as l:
                    for k in range(KT):
                        sp.wait_ge(s_used, l * KT + k + 1)
                        sp.dma_start(ada[k % ADA_BUFS][:, :], A["ada_w"][l, k * P:k * P + P, :])\
                            .then_inc(s_ada[k % ADA_BUFS], 16)

            @block.gpsimd
            def _(pool):
                for i in range(n_stacks):
                    nc.gpsimd.memset(row[i][:, :], 0.0).then_inc(s_zero, 1)
                nc.gpsimd.memset(core.ones[:, :], 1.0).then_inc(s_const, 1)
                nc.gpsimd.memset(core.eps[:, :], EPS).then_inc(s_const, 1)
                nc.gpsimd.memset(core.rg_par[:, :, :], 0.0).then_inc(s_const, 1)
                for t in core.carried:
                    nc.gpsimd.memset(t[:, :, :], 0.0)
                nc.gpsimd.memset(core.ident[:, :], 0.0).then_inc(s_const, 1)
                pool.wait_ge(s_const, 4)
                nc.gpsimd.affine_select(out=core.ident[:, :], in_=core.ident[:, :], compare_op=ALU.not_equal,
                                        fill=1.0, base=0, pattern=[[-1, P]], channel_multiplier=1)\
                    .then_inc(s_const, 1)

            @block.tensor
            def _(pe):
                pe.wait_ge(s_const, 5)
                pe.wait_ge(s_row, 16 * len(loads))
                for i in range(n_stacks):
                    nc.tensor.transpose(core.bank[i][:, 0:P], row[i][:, :], core.ident[:, :]).then_inc(s_tr, 1)
                with pe.Fori(0, depth) as l:
                    pe.wait_ge(s_used, l * KT + (ADA_BUFS + KT))
                    for m in range(24):
                        ins = nc.tensor.matmul(core.bank[7][:, bass.ds(l * 24 + m, 1)], acc[:, m * P:m * P + P],
                                               core.ones[:, 0:1], start=True, stop=True)
                    ins.then_inc(s_acc, 1)

            @block.scalar
            def _(act):
                act.wait_ge(s_col, 2)
                nc.scalar.activation(cond_t[:, :], core.col1[:, r1["c"]:r1["c"] + 8], ACT.Tanh, scale=0.5)\
                    .then_inc(s_tanh, 1)
                nc.scalar.activation(lam[:, 0, :], core.col1[:, r1["rg_lambda"]:r1["rg_lambda"] + 8], ACT.Exp,
                                     scale=-1.0).then_inc(s_tanh, 1)
                act.wait_ge(s_dve, 1)
                nc.scalar.activation(lam[:, 2, :], lam[:, 1, :], ACT.Ln).then_inc(s_tanh, 1)

            @block.vector
            def _(dve):
                st = Steps(dve, s_dve)
                for i, dst in enumerate([col0, core.col1] + ([core.dn_par] if n_stacks > 2 else [])):
                    dve.wait_ge(s_tr, i + 1)
                    nc.vector.tensor_copy(dst[:, :], core.bank[i][:, 0:P]).then_inc(s_col, 1)
                dve.wait_ge(s_col, n_stacks)
                dve.wait_ge(s_tanh, 2)
                e, w, ln, fix = (lam[:, i, :] for i in range(4))
                st.done(nc.vector.tensor_scalar(w, e, 1.0, None, op0=ALU.add))
                nc.vector.scalar_tensor_tensor(cond[:, :], cond_t[:, :], 1.0, core.col1[:, r1["c"]:r1["c"] + 8],
                                               op0=ALU.add, op1=ALU.mult).then_inc(s_dve, 1)
                dve.wait_ge(s_dve, 2)
                nc.vector.tensor_scalar(cond[:, :], cond[:, :], 0.5, None, op0=ALU.mult).then_inc(s_cond, 1)
                st.n = 2
                st.done(nc.vector.tensor_scalar(fix, w, -1.0, None, op0=ALU.add))
                st.done(nc.vector.tensor_tensor(fix, e, fix, ALU.subtract))
                dve.wait_ge(s_tanh, 3)
                st.done(nc.vector.reciprocal(w, w))
                st.done(nc.vector.tensor_tensor(fix, fix, w, ALU.mult))
                st.done(nc.vector.tensor_tensor(ln, ln, fix, ALU.add))
                dve.wait_ge(s_const, 5)
                rp = core.rg_par
                for i in range(4):
                    st.done(nc.vector.tensor_copy(rp[:, :, i], core.col1[:, r1["rg_conv_w"] + 8 * i:r1["rg_conv_w"] + 8 * i + 8]))
                st.done(nc.vector.tensor_copy(rp[:, :, 4], core.col1[:, r1["rg_conv_b"]:r1["rg_conv_b"] + 8]))
                for g in range(2):
                    st.done(nc.vector.tensor_scalar(rp[:, :, 5 + g], core.col1[:, r1["rg_gate_b"] + 8 * g:r1["rg_gate_b"] + 8 * g + 8],
                                                    0.5, None, op0=ALU.mult))
                st.done(nc.vector.tensor_scalar(rp[:, :, 7], ln, 4.0, None, op0=ALU.mult))
                st.done(nc.vector.tensor_scalar(rp[:, :, 8], ln, -4.0, None, op0=ALU.mult))
                st.done(nc.vector.tensor_copy(core.final_w[:, :], core.col1[:, r1["final"]:r1["final"] + 8]))
                dve.wait_ge(s_cond, 1)
                dve.sem_inc(s_used, ADA_BUFS)
                dve.sem_inc(s_acc, 1)
                with dve.Fori(0, depth) as l:
                    for k in range(KT):
                        dve.wait_ge(s_ada[k % ADA_BUFS], l * (16 * KT // ADA_BUFS) + (16 * (k // ADA_BUFS) + 16))
                        dve.wait_ge(s_used, l * KT + (ADA_BUFS + k))
                        if k == 0:
                            dve.wait_ge(s_acc, l + 1)
                            nc.vector.tensor_scalar(acc[:, :], ada[0][:, :], cond[:, 0:1], None, op0=ALU.mult)\
                                .then_inc(s_used, 1)
                        else:
                            nc.vector.scalar_tensor_tensor(acc[:, :], ada[k % ADA_BUFS][:, :], cond[:, k:k + 1], acc[:, :],
                                                           op0=ALU.mult, op1=ALU.add).then_inc(s_used, 1)
                dve.wait_ge(s_acc, depth + 1)
                st.done(nc.vector.tensor_tensor(mod[:, :], core.bank[7][:, 0:depth * 24], col0[:, 0:depth * 24], ALU.add))
                for l in range(depth):
                    shift, scale, gate = (mod[:, l * 24 + 8 * i:l * 24 + 8 * i + 8] for i in range(3))
                    here = slice(l * KT, l * KT + KT)
                    st.done(nc.vector.scalar_tensor_tensor(core.modA[:, here], scale, 1.0, col0[:, depth * 24 + 8 * l:depth * 24 + 8 * l + 8],
                                                           op0=ALU.add, op1=ALU.mult))
                    st.done(nc.vector.tensor_copy(core.modB[:, here], shift))
                    st.done(nc.vector.tensor_copy(core.modG[:, here], gate))


NHF = 4


def residual_phase(core, A, half, layer, depth):
    core.begin_phase()
    nc = core.nc
    ingest, final = layer < 0, layer == depth - 1
    tag = f"res{half}_{layer + 1}"
    nxt = slice((layer + 1) * KT, (layer + 2) * KT)
    h_hi, h_lo, x, y = core.h_hi, core.h_lo, core.x, core.y
    with ExitStack() as ctx:
        sq = [core.sb(f"{tag}_sq{i}", [P, CH], F32, ctx) for i in range(2)]
        rstd = core.sb(f"{tag}_rstd", [P, CH], F32, ctx)
        logv = core.sb(f"{tag}_log", [P, CH], F32, ctx)
        hf = [core.sb(f"{tag}_h{i}", [P, CH], F32, ctx) for i in range(NHF)]
        if ingest:
            xin = core.sb(f"{tag}_xin", [P, HALF // P, D], F32, ctx)
            s_in = [core.sem(f"{tag}_x_loaded{c}") for c in range(NCH)]
            projected, credit = core.sem(f"{tag}_x_transposed"), 0
        else:
            w = Weights(core, ctx, tag, 2)
            projected, credit = w.projected, 2
            s_yhi = core.sem(f"{tag}_y_rounded")
            s_ylo = [core.sem(f"{tag}_y_split{i}") for i in range(2)]
        if final:
            stage = [core.sb(f"{tag}_stage{i}", [P, D], F32, ctx) for i in range(2)]
            s_norm = core.sem(f"{tag}_normalized")
            s_tout = core.sem(f"{tag}_out_transposed")
            s_stage = core.sem(f"{tag}_staged")
            s_out = [core.sem(f"{tag}_out_stored{i}") for i in range(2)]
        s_x = core.sem(f"{tag}_x_updated")
        s_sq = core.sem(f"{tag}_squared")
        s_sum = core.sem(f"{tag}_summed")
        s_log = core.sem(f"{tag}_log_ready")
        s_r = core.sem(f"{tag}_rstd_ready")
        s_t = core.sem(f"{tag}_x_scaled")
        s_hf = core.sem(f"{tag}_h_ready")
        s_hi = core.sem(f"{tag}_h_rounded")
        s_lo = [core.sem(f"{tag}_h_split{i}") for i in range(2)]
        cs = [slice(c * CH, c * CH + CH) for c in range(NCH)]
        steps = [(c, d) for c in range(NCH) for d in range(KT)]

        with nc.Block() as block:
            @block.sync
            def _(sp):
                core.clear_last_phase(sp)
                if ingest:
                    for t in range(HALF // P):
                        at = half * HALF + t * P
                        sp.dma_start(xin[:, t, :], A["x"][0, at:at + P, :]).then_inc(s_in[t // 4], 16)
                else:
                    for j, (c, d) in enumerate(steps):
                        w.load(sp, wtile(core.w_out[layer], slice(d * P, d * P + P)), j)
                if final:
                    for t in range(HALF // P):
                        sp.wait_ge(s_stage, 2 * t + 2)
                        at = half * HALF + t * P
                        sp.dma_start(A["out"][0, at:at + P, :], stage[t % 2][:, :]).then_inc(s_out[t % 2], 16)
                    for i in range(2):
                        sp.wait_ge(s_out[i], 16 * (HALF // P // 2))

            @block.tensor
            def _(pe):
                if not ingest:
                    pe.sem_inc(w.projected, 2)

                def sum_squares(j):
                    c, d = steps[j]
                    pe.wait_ge(s_sq, j + 1)
                    nc.tensor.matmul(core.bank[4 + c][:, :], core.ones[:, :], sq[j % 2][:, :],
                                     start=(d == 0), stop=(d == KT - 1)).then_inc(s_sum, 1)

                for j, (c, d) in enumerate(steps):
                    if j >= 2:
                        pe.wait_ge(s_x, j - 1)
                    if ingest:
                        if d == 0:
                            pe.wait_ge(s_in[c], 16 * 4)
                        for t in range(4):
                            ins = nc.tensor.transpose(core.bank[j % 2][:, t * P:t * P + P],
                                                      xin[:, 4 * c + t, d * P:d * P + P], core.ident[:, :])
                        ins.then_inc(projected, 1)
                    else:
                        w.multiply(pe, core.bank[j % 2][:, :], j, h_hi, h_lo, cs[c],
                                   each_k=[(s_ylo[k % 2], (KT * c + k) // 2 + 1) for k in range(KT)] if d == 0 else None)
                    if j >= 1:
                        sum_squares(j - 1)
                sum_squares(len(steps) - 1)
                if final:
                    for t in range(HALF // P):
                        c = t // 4
                        for g in range(2):
                            n = 2 * t + g
                            pe.wait_ge(s_norm, 8 * c + 4 * g + 4)
                            if n >= 2:
                                pe.wait_ge(s_stage, n - 1)
                            for k in range(4):
                                ins = nc.tensor.transpose(core.bank[6 + n % 2][:, k * P:k * P + P],
                                                          x[:, 4 * g + k, t * P:t * P + P], core.ident[:, :])
                            ins.then_inc(s_tout, 1)

            def norm_dve(dve, c, k):
                m = c * KT + k
                if k == 0:
                    dve.wait_ge(s_r, c + 1)
                if final:
                    nc.vector.scalar_tensor_tensor(x[:, k, cs[c]], x[:, k, cs[c]], core.final_w[:, k:k + 1],
                                                   rstd[:, :], op0=ALU.mult, op1=ALU.mult).then_inc(s_norm, 1)
                    return
                if m >= NHF:
                    dve.wait_ge(s_lo[m % 2], (m - NHF) // 2 + 1)
                nc.vector.tensor_tensor(hf[m % NHF][:, :], x[:, k, cs[c]], rstd[:, :], ALU.mult).then_inc(s_t, 1)
                if m % 2:
                    norm_low(dve, nc.vector, m - 1)

            def norm_low(eng, alu, m):
                c, k = m // KT, m % KT
                eng.wait_ge(s_hi, m + 1)
                alu.tensor_tensor(h_lo[:, k, cs[c]], hf[m % NHF][:, :], h_hi[:, k, cs[c]].bitcast(F32),
                                  ALU.subtract).then_inc(s_lo[m % 2], 1)

            def norm_act(act, c, k):
                m = c * KT + k
                if final:
                    return
                if k == 0 and not ingest:
                    act.wait_ge(projected, credit + 8 * (c + 1))
                act.wait_ge(s_t, m + 1)
                col = (layer + 1) * KT + k
                nc.scalar.activation(hf[m % NHF][:, :], hf[m % NHF][:, :], ACT.Identity, scale=core.modA[:, col:col + 1],
                                     bias=core.modB[:, col:col + 1]).then_inc(s_hf, 1)
                act.wait_ge(s_hf, m + 1)
                nc.scalar.activation(h_hi[:, k, cs[c]], hf[m % NHF][:, :], ACT.Copy).then_inc(s_hi, 1)

            def norm_pool(pool, c, k):
                if not final and k % 2:
                    norm_low(pool, nc.gpsimd, c * KT + k)

            def y_low(eng, alu, c, k):
                eng.wait_ge(s_yhi, c * KT + k + 1)
                alu.tensor_tensor(h_lo[:, k, cs[c]], y[:, k, cs[c]], h_hi[:, k, cs[c]].bitcast(F32), ALU.subtract)\
                    .then_inc(s_ylo[k % 2], 1)

            @block.vector
            def _(dve):
                if not ingest:
                    for k in range(0, KT, 2):
                        y_low(dve, nc.vector, 0, k)
                for j, (c, d) in enumerate(steps):
                    if not ingest and c + 1 < NCH and d % 2 == 0:
                        y_low(dve, nc.vector, c + 1, d)
                    dve.wait_ge(projected, credit + j + 1)
                    here = x[:, d, cs[c]]
                    if ingest:
                        ins = nc.vector.tensor_copy(here, core.bank[j % 2][:, :])
                    else:
                        col = layer * KT + d
                        ins = nc.vector.scalar_tensor_tensor(here, core.bank[j % 2][:, :], core.modG[:, col:col + 1],
                                                             here, op0=ALU.mult, op1=ALU.add)
                    ins.then_inc(s_x, 1)
                    if c > 0:
                        norm_dve(dve, c - 1, d)
                for k in range(KT):
                    norm_dve(dve, NCH - 1, k)
                if final:
                    for n in range(2 * (HALF // P)):
                        t, g = n // 2, n % 2
                        dve.wait_ge(s_tout, n + 1)
                        if t >= 2 and g == 0:
                            dve.wait_ge(s_out[t % 2], 16 * (t // 2))
                        nc.vector.tensor_copy(stage[t % 2][:, g * CH:g * CH + CH], core.bank[6 + n % 2][:, :])\
                            .then_inc(s_stage, 1)

            @block.scalar
            def _(act):
                def split_y(c, k):
                    nc.scalar.activation(h_hi[:, k, cs[c]], y[:, k, cs[c]], ACT.Copy).then_inc(s_yhi, 1)

                if not ingest:
                    w.round(act, 0, 1)
                    for k in range(KT):
                        split_y(0, k)
                    w.round(act, 1, 2)
                for j, (c, d) in enumerate(steps):
                    if not ingest and j + 2 < len(steps):
                        w.round(act, j + 2, j + 3)
                    if not ingest and c + 1 < NCH:
                        split_y(c + 1, d)
                    act.wait_ge(s_x, j + 1)
                    if j >= 2:
                        act.wait_ge(s_sum, j - 1)
                    nc.scalar.activation(sq[j % 2][:, :], x[:, d, cs[c]], ACT.Square).then_inc(s_sq, 1)
                    if c > 0:
                        norm_act(act, c - 1, d)
                    if d == KT - 1:
                        act.wait_ge(s_sum, j + 1)
                        nc.scalar.activation(logv[:, :], core.bank[4 + c][:, :], ACT.Ln, bias=core.eps[:, 0:1],
                                             scale=1.0 / D).then_inc(s_log, 1)
                        act.wait_ge(s_log, c + 1)
                        if c > 0:
                            act.wait_ge(s_norm if final else s_t, KT * c)
                        nc.scalar.activation(rstd[:, :], logv[:, :], ACT.Exp, scale=-0.5).then_inc(s_r, 1)
                for k in range(KT):
                    norm_act(act, NCH - 1, k)

            @block.gpsimd
            def _(pool):
                if not ingest:
                    pool.sem_inc(w.split, 2)
                    w.subtract(pool, 0)
                    for k in range(1, KT, 2):
                        y_low(pool, nc.gpsimd, 0, k)
                    w.subtract(pool, 1)
                for j, (c, d) in enumerate(steps):
                    if not ingest and j + 2 < len(steps):
                        w.subtract(pool, j + 2)
                    if not ingest and c + 1 < NCH and d % 2:
                        y_low(pool, nc.gpsimd, c + 1, d)
                    if c > 0:
                        norm_pool(pool, c - 1, d)
                for k in range(KT):
                    norm_pool(pool, NCH - 1, k)


def rg_phase(core, A, half):
    core.begin_phase()
    nc = core.nc
    tag = f"rg{half}"
    T, S = 2, 4
    h_hi, h_lo, y, par = core.h_hi, core.h_lo, core.y, core.rg_par
    w_in = A["rg_w_in"][0]
    gate_w_v = A["rg_gate_w"][0].rearrange("n k g j -> k n (g j)")
    with ExitStack() as ctx:
        w = Weights(core, ctx, tag, S)

        def two(name, width=CH):
            return [core.sb(f"{tag}_{name}{i}", [P, width], F32, ctx) for i in range(2)]
        gw = two("gate_w", 256)
        cur = two("params", 13)
        u_in = two("u_in", CH + 3)
        u = two("u")
        r = two("r")
        a = two("a")
        mult = two("mult")
        inp = two("inp")
        sil = two("silu")
        hs = r
        asq = r
        s_gw = [core.sem(f"{tag}_gate_w_loaded{i}") for i in range(2)]
        s_uc = core.sem(f"{tag}_u_copied")
        s_conv = core.sem(f"{tag}_convolved")
        s_gates = core.sem(f"{tag}_gates_multiplied")
        s_rt = core.sem(f"{tag}_r_ready")
        s_a = core.sem(f"{tag}_a_ready")
        s_th = core.sem(f"{tag}_tanh_ready")
        s_asq = core.sem(f"{tag}_a_squared")
        s_i = core.sem(f"{tag}_i_ready")
        s_g = core.sem(f"{tag}_gate_ready")
        s_m2 = core.sem(f"{tag}_mult_squared")
        s_m = core.sem(f"{tag}_mult_ready")
        s_dve = core.sem(f"{tag}_dve")
        s_end = core.sem(f"{tag}_tile_ended")
        DVE_STEPS = 40

        with nc.Block() as block:
            @block.sync
            def _(sp):
                core.clear_last_phase(sp)
                with sp.Fori(0, KT // 2) as it:
                    for nn in range(2):
                        for t in range(T):
                            w.load(sp, wtile(w_in, bass.ds(it * (2 * P) + (nn * P + t * D), P)), nn * T + t, it * (2 * T))
                        sp.wait_ge(s_end, it * 2 + nn + 1)
                        sp.dma_start(gw[nn][:, :], gate_w_v[:, it * 2 + nn, :]).then_inc(s_gw[nn], 16)

            @block.gpsimd
            def _(pool):
                pool.sem_inc(w.split, 2)
                with pool.Fori(0, KT // 2) as it:
                    for nn in range(2):
                        for t in range(T):
                            w.subtract(pool, nn * T + t, it * (2 * T))

            @block.tensor
            def _(pe):
                pe.sem_inc(w.projected, 2 * S)

                def body(it, last):
                    for nn in range(2):
                        for c in range(NCH):
                            unit = nn * NCH + c
                            cols = slice(c * CH, c * CH + CH)
                            w.multiply(pe, core.bank[c][:, :], nn * T, h_hi, h_lo, cols, it * (2 * T))
                            w.multiply(pe, core.bank[2 + c][:, :], nn * T + 1, h_hi, h_lo, cols, it * (2 * T))
                            if c == 0:
                                pe.wait_ge(s_gw[nn], 16 * it + 16)
                            pe.wait_ge(s_conv, it * 4 + unit + 1)
                            nc.tensor.matmul(core.bank[4 + c][:, :], gw[nn][:, 0:P], u[c][:, :], start=True, stop=True)\
                                .then_inc(s_gates, 1)
                            nc.tensor.matmul(core.bank[6 + c][:, :], gw[nn][:, P:2 * P], u[c][:, :], start=True,
                                             stop=True).then_inc(s_gates, 1)
                each(pe, KT // 2, body)

            @block.scalar
            def _(act):
                def round_tiles(nn, it):
                    for t in range(T):
                        j = nn * T + t
                        w.round(act, j, it * 8 + nn * 4 + T + t + 1, arrivals=it * (16 * T))

                round_tiles(0, 0)

                def body(it, last):
                    for nn in range(2):
                        for c in range(NCH):
                            unit = nn * NCH + c
                            now = it * 4 + unit + 1
                            act.wait_ge(w.projected, it * 8 + (2 * S + unit * T + 1))
                            nc.scalar.activation(u_in[c][:, 3:CH + 3], core.bank[c][:, :], ACT.Copy).then_inc(s_uc, 1)
                            if c == 0 and nn == 0:
                                round_tiles(1, it)
                            if c == 0 and nn == 1 and not last:
                                round_tiles(0, it + 1)
                            act.wait_ge(s_gates, it * 8 + unit * 2 + 1)
                            nc.scalar.activation(r[c][:, :], core.bank[4 + c][:, :], ACT.Tanh, scale=0.5,
                                                 bias=cur[nn][:, 5:6]).then_inc(s_rt, 1)
                            act.wait_ge(s_rt, now)
                            nc.scalar.activation(a[c][:, :], r[c][:, :], ACT.Exp, scale=cur[nn][:, 8:9],
                                                 bias=cur[nn][:, 8:9]).then_inc(s_a, 1)
                            nc.scalar.activation(mult[c][:, :], r[c][:, :], ACT.Tanh, scale=cur[nn][:, 7:8],
                                                 bias=cur[nn][:, 7:8]).then_inc(s_th, 1)
                            act.wait_ge(s_a, now)
                            act.wait_ge(s_th, now)
                            nc.scalar.activation(asq[c][:, :], a[c][:, :], ACT.Square).then_inc(s_asq, 1)
                            act.wait_ge(s_gates, it * 8 + unit * 2 + 2)
                            nc.scalar.activation(inp[c][:, :], core.bank[6 + c][:, :], ACT.Tanh, scale=0.5,
                                                 bias=cur[nn][:, 6:7]).then_inc(s_i, 1)
                            act.wait_ge(w.projected, it * 8 + (2 * S + unit * T + 2))
                            nc.scalar.activation(sil[c][:, :], core.bank[2 + c][:, :], ACT.Tanh, scale=0.5)\
                                .then_inc(s_g, 1)
                            act.wait_ge(s_m2, now)
                            nc.scalar.activation(mult[c][:, :], mult[c][:, :], ACT.Sqrt, scale=0.25).then_inc(s_m, 1)
                each(act, KT // 2, body)

            @block.vector
            def _(dve):
                dve.sem_inc(s_end, 2)

                def body(it, last):
                    st = Steps(dve, s_dve, it * DVE_STEPS)
                    for nn in range(2):
                        st.done(nc.vector.tensor_copy(cur[nn][:, :], par[:, it * 2 + nn, :]))
                        for c in range(NCH):
                            unit = nn * NCH + c
                            now = it * 4 + unit + 1
                            halo = cur[nn][:, 9:12] if c == 0 else u_in[0][:, CH:CH + 3]
                            st.done(nc.vector.tensor_copy(u_in[c][:, 0:3], halo))
                            dve.wait_ge(s_uc, now)
                            st.done(nc.vector.tensor_scalar(u[c][:, :], u_in[c][:, 3:CH + 3], cur[nn][:, 3:4],
                                                            cur[nn][:, 4:5], op0=ALU.mult, op1=ALU.add))
                            for k in range(3):
                                ins = nc.vector.scalar_tensor_tensor(u[c][:, :], u_in[c][:, k:k + CH], cur[nn][:, k:k + 1],
                                                                     u[c][:, :], op0=ALU.mult, op1=ALU.add)
                                if k < 2:
                                    st.done(ins)
                            ins.then_inc(s_conv, 1)
                            dve.wait_ge(s_conv, now)
                            dve.wait_ge(s_th, now)
                            dve.wait_ge(s_asq, now)
                            nc.vector.scalar_tensor_tensor(mult[c][:, :], asq[c][:, :], 1.0, mult[c][:, :],
                                                           op0=ALU.add, op1=ALU.mult).then_inc(s_m2, 1)
                            dve.wait_ge(s_i, now)
                            st.done(nc.vector.scalar_tensor_tensor(inp[c][:, :], inp[c][:, :], 1.0, u[c][:, :],
                                                                   op0=ALU.add, op1=ALU.mult))
                            dve.wait_ge(s_g, now)
                            st.done(nc.vector.scalar_tensor_tensor(sil[c][:, :], sil[c][:, :], 1.0, core.bank[2 + c][:, :],
                                                                   op0=ALU.add, op1=ALU.mult))
                            dve.wait_ge(s_m, now)
                            st.done(nc.vector.tensor_tensor(inp[c][:, :], inp[c][:, :], mult[c][:, :], ALU.mult))
                            first = cur[nn][:, 12:13] if c == 0 else hs[0][:, CH - 1:CH]
                            st.done(nc.vector.tensor_tensor_scan(hs[c][:, :], a[c][:, :], inp[c][:, :], first,
                                                                 ALU.mult, ALU.add))
                            st.done(nc.vector.scalar_tensor_tensor(y[:, it * 2 + nn, c * CH:c * CH + CH], sil[c][:, :], 0.5,
                                                                   hs[c][:, :], op0=ALU.mult, op1=ALU.mult))
                        st.done(nc.vector.tensor_copy(par[:, it * 2 + nn, 9:12], u_in[1][:, CH:CH + 3]))
                        nc.vector.tensor_copy(par[:, it * 2 + nn, 12:13], hs[1][:, CH - 1:CH]).then_inc(s_end, 1)
                    assert st.n == DVE_STEPS, st.n
                each(dve, KT // 2, body)


H = 8
NB = HALF // P
LEVELS = (2, 4, 8, 16, 32, 64)


def bcast_last(ap, n):
    return ap.unsqueeze(2).broadcast_to([ap.shape[0], ap.shape[1], n])


def bcast_mid(ap, n):
    return ap.unsqueeze(1).broadcast_to([ap.shape[0], n, ap.shape[1]])


def dn_project_phase(core, A, half):
    core.begin_phase()
    nc = core.nc
    tag = f"dnp{half}"
    T = S = 4
    h_hi, h_lo = core.h_hi, core.h_lo
    w_in = A["dn_w_in"][0]
    halo, qkvz = core.dn_halo, core.dn_qkvz
    taps = core.dn_par[:, 0:96].rearrange("p (k i n) -> p k i n", k=4, i=3)
    with ExitStack() as ctx:
        w = Weights(core, ctx, tag, S)
        raw = [core.sb(f"{tag}_raw{i}", [P, CH + 3], F32, ctx) for i in range(3)]
        conv = [core.sb(f"{tag}_conv{i}", [P, CH], F32, ctx) for i in range(3)]
        out = [[core.y[:, i, c * CH:c * CH + CH] for c in range(NCH)] for i in range(4)]
        sq = [core.y[:, 4 + i, 0:CH] for i in range(2)]
        cur = core.sb(f"{tag}_taps", [P, 4, 3], F32, ctx)
        wab = core.sb(f"{tag}_wab", [P, KT, 16], F32, ctx)
        wab_hi = core.sb(f"{tag}_wab_hi", [P, KT, 16], F32R, ctx)
        wab_lo = core.sb(f"{tag}_wab_lo", [P, KT, 16], F32R, ctx)
        s_ab = core.sem(f"{tag}_ab_loaded")
        s_abh = core.sem(f"{tag}_ab_rounded")
        s_abl = core.sem(f"{tag}_ab_split")
        s_abc = core.sem(f"{tag}_ab_copied")
        abT = core.y[0:16, 6, :]
        s_abp = core.sem(f"{tag}_ab_multiplied")
        s_head = core.sem(f"{tag}_halo_ready")
        s_raw = core.sem(f"{tag}_raw_copied")
        s_conv = core.sem(f"{tag}_convolved")
        s_th = core.sem(f"{tag}_tanh_ready")
        s_zth = core.sem(f"{tag}_z_tanh_ready")
        s_out = core.sem(f"{tag}_silu_ready")
        s_sq = core.sem(f"{tag}_squared")
        s_sum = core.sem(f"{tag}_summed")
        s_dve = core.sem(f"{tag}_dve")
        s_st = [[core.sem(f"{tag}_stored{i}_{c}") for c in range(NCH)] for i in range(4)]
        DVE_STEPS = 1 + 2 * 9 + 3

        with nc.Block() as block:
            @block.sync
            def _(sp):
                core.clear_last_phase(sp)
                sp.dma_start(wab[:, :, :], w_in.rearrange("(t p) n -> p t n", p=P)[:, :, 4 * D:4 * D + 16])\
                    .then_inc(s_ab, 16)

                def store(i, c, n):
                    sp.wait_ge(s_out, n * 8 + (4 + c * 4 + i + 1))
                    sp.dma_start(qkvz[i, n, :, c * CH:c * CH + CH], out[i][c][:, :]).then_inc(s_st[i][c], 16)

                for t in range(T):
                    w.load(sp, wtile(w_in, slice(t * D, t * D + P)), t)

                def body(n, last):
                    for i in range(4):
                        if not last and i % 2 == 0:
                            w.load(sp, wtile(w_in, bass.ds(n * P + (P + i // 2 * D), P)), i // 2, n * T + T)
                        store(i, 0, n)
                    for i in range(4):
                        if not last and i % 2 == 0:
                            w.load(sp, wtile(w_in, bass.ds(n * P + (P + (2 + i // 2) * D), P)), 2 + i // 2, n * T + T)
                        store(i, 1, n)
                each(sp, H, body)
                for i in range(4):
                    for c in range(NCH):
                        sp.wait_ge(s_st[i][c], 16 * (H + 1))

            @block.gpsimd
            def _(pool):
                pool.sem_inc(w.split, 2)
                pool.wait_ge(s_abh, 1)
                nc.gpsimd.tensor_tensor(wab_lo[:, :, :], wab[:, :, :], wab_hi[:, :, :].bitcast(F32), ALU.subtract)\
                    .then_inc(s_abl, 1)
                for i in range(4):
                    for c in range(NCH):
                        pool.sem_inc(s_st[i][c], 16)

                with pool.Fori(0, H) as n:
                    for t in range(T):
                        w.subtract(pool, t, n * T)

            @block.tensor
            def _(pe):
                pe.sem_inc(w.projected, 2 * S)
                pe.wait_ge(s_abl, 1)
                for c in range(NCH):
                    for k in range(KT):
                        for m, (x, ww) in enumerate(((h_hi, wab_hi), (h_hi, wab_lo), (h_lo, wab_hi))):
                            ins = nc.tensor.matmul(core.bank[6 + c][0:16, :], ww[:, k, :], x[:, k, c * CH:c * CH + CH],
                                                   start=(k == 0 and m == 0), stop=(k == KT - 1 and m == 2))
                    ins.then_inc(s_abp, 1)
                pe.wait_ge(s_abc, NCH)
                for b in range(NB):
                    ins = nc.tensor.transpose(core.bank[5][:, 16 * b:16 * b + 16], abT[:, b * P:b * P + P],
                                              core.ident[0:16, 0:16])
                ins.then_inc(s_abp, 1)

                def body(n, last):
                    def sums(c):
                        for i in range(2):
                            pe.wait_ge(s_sq, n * 4 + (4 + c * 2 + i + 1))
                            for b in range(4):
                                col = n + (i * 64 + (4 * c + b) * H)
                                ins = nc.tensor.matmul(core.bank[4][:, bass.ds(col, 1)], sq[i][:, b * P:b * P + P],
                                                       core.ones[:, 0:1], start=True, stop=True)
                            ins.then_inc(s_sum, 1)

                    for c in range(NCH):
                        cols = slice(c * CH, c * CH + CH)
                        for t in range(T):
                            if t < 3:
                                pe.wait_ge(s_raw, n * 6 + (c * 3 + t + 1))
                            else:
                                pe.wait_ge(s_out, n * 8 + (4 * c + 4))
                            w.multiply(pe, core.bank[t][:, :], t, h_hi, h_lo, cols, n * T)
                            if c == 1 and t == 1:
                                sums(0)
                    sums(1)
                pe.sem_inc(s_raw, 3)
                pe.sem_inc(s_out, 4)
                each(pe, H, body)

            @block.scalar
            def _(act):
                act.wait_ge(s_ab, 16)
                nc.scalar.activation(wab_hi[:, :, :], wab[:, :, :], ACT.Copy).then_inc(s_abh, 1)

                def round_tile(t, n):
                    w.round(act, t, n * 8 + (T + t + 1), arrivals=n * (8 * T))

                for t in range(T):
                    round_tile(t, 0)

                def tanh(i, c, n):
                    act.wait_ge(s_conv, n * 6 + (c * 3 + i + 1))
                    act.wait_ge(s_st[i][c], n * 16 + 16)
                    if i < 2:
                        act.wait_ge(s_sq, n * 4 + (2 * c + i + 1))
                    nc.scalar.activation(out[i][c][:, :], conv[i][:, :], ACT.Tanh, scale=0.5).then_inc(s_th, 1)

                def body(n, last):
                    for c in range(NCH):
                        for i in range(3):
                            act.wait_ge(w.projected, n * 8 + (2 * S + c * T + i + 1))
                            act.wait_ge(s_head, n * 6 + (c * 3 + i + 1))
                            nc.scalar.activation(raw[i][:, 3:CH + 3], core.bank[i][:, :], ACT.Copy).then_inc(s_raw, 1)
                            if c == 1 and not last:
                                round_tile(i, n + 1)
                            if i > 0:
                                tanh(i - 1, c, n)
                        tanh(2, c, n)
                        for m in range(2):
                            act.wait_ge(s_out, n * 8 + (4 + c * 4 + m + 1))
                            act.wait_ge(s_sum, n * 4 + (c * 2 + m + 1))
                            nc.scalar.activation(sq[m][:, :], out[m][c][:, :], ACT.Square).then_inc(s_sq, 1)
                        act.wait_ge(w.projected, n * 8 + (2 * S + c * T + 4))
                        act.wait_ge(s_st[3][c], n * 16 + 16)
                        nc.scalar.activation(out[3][c][:, :], core.bank[3][:, :], ACT.Tanh, scale=0.5)\
                            .then_inc(s_zth, 1)
                    if not last:
                        round_tile(3, n + 1)
                act.sem_inc(s_sq, 4)
                each(act, H, body)

            @block.vector
            def _(dve):
                dve.sem_inc(s_sum, 2)
                for c in range(NCH):
                    dve.wait_ge(s_abp, c + 1)
                    nc.vector.tensor_copy(abT[:, c * CH:c * CH + CH], core.bank[6 + c][0:16, :]).then_inc(s_abc, 1)
                dve.wait_ge(s_abp, NCH + 1)
                nc.vector.tensor_copy(core.dn_ab[:, :], core.bank[5][:, 0:P]).then_inc(s_abp, 1)
                for i in range(3):
                    nc.vector.tensor_copy(raw[i][:, 0:3], halo[:, i, 0, :]).then_inc(s_head, 1)

                def body(n, last):
                    st = Steps(dve, s_dve, n * DVE_STEPS)
                    st.done(nc.vector.tensor_copy(cur[:, :, :], taps[:, :, :, n]))
                    for c in range(NCH):
                        def convolve(i):
                            dve.wait_ge(s_raw, n * 6 + (3 + c * 3 + i + 1))
                            dve.wait_ge(s_out, n * 8 + (c * 4 + i + 1))
                            st.done(nc.vector.tensor_scalar(conv[i][:, :], raw[i][:, 3:CH + 3], cur[:, 3, i:i + 1], None,
                                                            op0=ALU.mult))
                            for k in range(3):
                                ins = nc.vector.scalar_tensor_tensor(conv[i][:, :], raw[i][:, k:k + CH], cur[:, k, i:i + 1],
                                                                     conv[i][:, :], op0=ALU.mult, op1=ALU.add)
                                if k < 2:
                                    st.done(ins)
                            ins.then_inc(s_conv, 1)
                            dve.wait_ge(s_conv, n * 6 + (c * 3 + i + 1))
                            if c == 1:
                                st.done(nc.vector.tensor_copy(halo[:, i, n, :], raw[i][:, CH:CH + 3]))
                            if c == 0:
                                nc.vector.tensor_copy(raw[i][:, 0:3], raw[i][:, CH:CH + 3]).then_inc(s_head, 1)
                            elif not last:
                                nc.vector.tensor_copy(raw[i][:, 0:3], halo[:, i, n + 1, :]).then_inc(s_head, 1)

                        def double_silu(i):
                            dve.wait_ge(s_th, n * 6 + (c * 3 + i + 1))
                            nc.vector.scalar_tensor_tensor(out[i][c][:, :], out[i][c][:, :], 1.0, conv[i][:, :],
                                                           op0=ALU.add, op1=ALU.mult).then_inc(s_out, 1)
                        convolve(0)
                        convolve(1)
                        double_silu(0)
                        convolve(2)
                        double_silu(1)
                        double_silu(2)
                        dve.wait_ge(s_zth, n * 2 + (c + 1))
                        nc.vector.scalar_tensor_tensor(out[3][c][:, :], out[3][c][:, :], 1.0, core.bank[3][:, :],
                                                       op0=ALU.add, op1=ALU.mult).then_inc(s_out, 1)
                    assert st.n == DVE_STEPS, st.n
                each(dve, H, body)
                dve.wait_ge(s_sum, 2 + 4 * H)
                nc.vector.tensor_copy(core.dn_sums[:, :], core.bank[4][:, 0:P]).then_inc(s_abp, 1)


def dn_recur_phase(core, A, half):
    core.begin_phase()
    nc = core.nc
    tag = f"dnr{half}"
    y = core.y
    NK = 10
    GC, EGL, EDEC, KBES, BETA, VBS, RK, RQS, S2, G = range(NK)
    GRP = 2
    with ExitStack() as ctx:
        def big(name, cols=P):
            return core.sb(f"{tag}_{name}", [P, H, cols], F32, ctx)
        masks = core.sb(f"{tag}_masks", [P, 7 * P + 64], F32, ctx)
        upper = masks[:, 0:P]
        level_mask = {s: masks[:, (1 + n) * P:(2 + n) * P] for n, s in enumerate(LEVELS)}
        ident_c, mask1_c = masks[:, 7 * P:7 * P + 32], masks[:, 7 * P + 32:7 * P + 64]
        qT, kT, vT, zT = ([big(f"{n}{i}") for i in range(2)] for n in ("qT", "kT", "vT", "zT"))
        sA = core.sb(f"{tag}_scalars", [P, NK, NB, H], F32, ctx)
        cur = core.sb(f"{tag}_cur", [P, NK, H], F32, ctx)
        kn, knT, vb, kbe, kdec = big("kn"), big("knT"), big("vb"), big("kbe"), big("kdec")
        gu, e0, e1, eq, Am, at = big("gu"), big("e0"), big("e1"), big("eq"), big("A"), big("attnT")
        AL = {s: big(f"A{s}") for s in LEVELS}
        XF, YF, X2, Y2, PF = big("XF"), big("YF"), big("X2"), big("Y2"), big("PF")
        Xc, Yc, Pc = big("Xc", 32), big("Yc", 32), big("Pc", 32)
        nw, Sd, sqo, on, vn, qe = knT, gu, e0, e1, PF, eq
        small = core.sb(f"{tag}_small", [P, 8, NB * H], F32, ctx)
        tiny = core.sb(f"{tag}_tiny", [P, 4, H], F32, ctx)
        state = core.dn_state
        head_v = core.sb(f"{tag}_head_vectors", [P, 2, H], F32, ctx)
        eps4 = core.sb(f"{tag}_eps4", [P, 1], F32, ctx)
        nwcol = core.sb(f"{tag}_norm_w", [P, 1], F32, ctx)

        names = ("consts", "pre_act", "pre_dve", "pre_pe", "zeroed", "cur", "kt", "vt", "kn", "vb", "gu", "bc", "dd", "e0", "e1",
                 "e0x", "eqx", "e1x", "knt", "kntc", "m0", "m1", "qe", "g", "at", "A", "at2", "compact", "xf", "yc",
                 "al", "p", "pc", "q", "r", "w", "nw", "kbe", "kdec", "uv", "vn", "o", "kv", "sd", "state",
                 "sqo", "sqr", "var", "std", "rec", "f", "on", "ot", "y", "x1", "y16")
        s = {n: core.sem(f"{tag}_{n}") for n in names}
        s_ld = [core.sem(f"{tag}_loaded{i}") for i in range(2)]
        bank = core.bank

        def grp(t, g):
            return t[:, 4 * g:4 * g + 4, :]

        def bk(i, g, n=CH):
            return bank[i + 4 * g][:, 0:n].rearrange("p (h c) -> p h c", h=4)

        with nc.Block() as block:
            @block.sync
            def _(sp):
                core.clear_last_phase(sp)
                sp.dma_start(masks[:, :], A["delta_masks"]).then_inc(s["consts"], 16)
                sp.dma_start(head_v[:, 0, :], A["dn_a_log"].partition_broadcast(P)[:, 0, :]).then_inc(s["consts"], 16)
                sp.dma_start(head_v[:, 1, :], A["dn_dt_bias"].partition_broadcast(P)[:, 0, :]).then_inc(s["consts"], 16)
                with sp.Fori(0, NB // 2) as it:
                    for bb in range(2):
                        sp.wait_ge(s["y"], it * 4 + (2 * bb + 2))
                        for i, t in enumerate((qT, kT, vT, zT)):
                            src = core.dn_qkvz[i].rearrange("n p t -> p n t")[:, :, bass.ds(it * 256 + bb * P, P)]
                            sp.dma_start(t[bb][:, :, :], src).then_inc(s_ld[bb], 16)

            @block.tensor
            def _(pe):
                pe.wait_ge(s["consts"], 48)
                pe.wait_ge(s["pre_dve"], 13)
                nc.tensor.matmul(bank[0][:, 0:64], upper, small[:, 5, :], start=True, stop=True).then_inc(s["pre_pe"], 1)
                nc.tensor.matmul(bank[1][:, 0:64], core.ones[:, :], small[:, 5, :], start=True, stop=True)\
                    .then_inc(s["pre_pe"], 1)

                def turn_out(block):
                    for g in range(GRP):
                        pe.wait_ge(s["on"], block * 2 + (g + 3))
                        for n, h in enumerate(range(4 * g, 4 * g + 4)):
                            ins = nc.tensor.transpose(bank[1 + 4 * g][:, n * P:n * P + P], on[:, h, :], core.ident[:, :])
                        ins.then_inc(s["ot"], 1)

                def body(it, previous):
                    for bb in range(2):
                        def now(g, lvl=None, per=1):
                            extra = (lvl or 0) * 2
                            return it * (4 * per) + (bb * 2 * per + extra + g + 1)

                        def before(g):
                            return it * 4 + (bb * 2 + g + 1)

                        def heads(g):
                            return range(4 * g, 4 * g + 4)

                        pe.wait_ge(s_ld[bb], it * 64 + 64)
                        for g in range(GRP):
                            pe.wait_ge(s["vn"], before(g))
                            for n, h in enumerate(heads(g)):
                                ins = nc.tensor.transpose(bank[4 * g][:, n * P:n * P + P], kT[bb][:, h, :], core.ident[:, :])
                            ins.then_inc(s["kt"], 1)
                        if bb:
                            turn_out(it * 2)
                        elif previous is not None:
                            turn_out(previous * 2 + 1)
                        for g in range(GRP):
                            pe.wait_ge(s["y"], before(g) + 2)
                            for n, h in enumerate(heads(g)):
                                ins = nc.tensor.transpose(bank[1 + 4 * g][:, n * P:n * P + P], vT[bb][:, h, :], core.ident[:, :])
                            ins.then_inc(s["vt"], 1)
                        for g in range(GRP):
                            pe.wait_ge(s["gu"], now(g))
                            pe.wait_ge(s["state"], before(g))
                            nc.tensor.matmul(bank[3 + 4 * g][:, :], core.ones[:, :], grp(gu, g).rearrange("p h c -> p (h c)"),
                                             start=True, stop=True).then_inc(s["bc"], 1)
                        for g in range(GRP):
                            pe.wait_ge(s["kn"], now(g))
                            pe.wait_ge(s["on"], before(g))
                            for n, h in enumerate(heads(g)):
                                ins = nc.tensor.transpose(bank[2 + 4 * g][:, n * P:n * P + P], kn[:, h, :], core.ident[:, :])
                            ins.then_inc(s["knt"], 1)
                        for g in range(GRP):
                            pe.wait_ge(s["kntc"], now(g))
                            for n, h in enumerate(heads(g)):
                                ins = nc.tensor.matmul(bank[4 * g][:, n * P:n * P + P], knT[:, h, :], knT[:, h, :],
                                                       start=True, stop=True)
                            ins.then_inc(s["g"], 1)
                            pe.wait_ge(s["vb"], now(g))
                            for n, h in enumerate(heads(g)):
                                ins = nc.tensor.matmul(bank[1 + 4 * g][:, n * P:n * P + P], knT[:, h, :], qT[bb][:, h, :],
                                                       start=True, stop=True)
                            ins.then_inc(s["at"], 1)
                        for lvl, size in enumerate(LEVELS):
                            full = size >= 32
                            nn = P if full else 32
                            Yin, Pin = ((YF if size == 32 else Y2), PF) if full else (Yc, Pc)
                            Xin = X2 if size == 64 else XF
                            for g in range(GRP):
                                pe.wait_ge(s["al"], now(g, lvl, 6))
                                pe.wait_ge(s["yc"], now(g, lvl, 7))
                                if lvl == 0:
                                    pe.wait_ge(s["A"], now(g))
                                for n, h in enumerate(heads(g)):
                                    ins = nc.tensor.matmul(bank[4 * g][:, n * nn:n * nn + nn], AL[size][:, h, :], Yin[:, h, :],
                                                           start=True, stop=True)
                                ins.then_inc(s["p"], 1)
                            for g in range(GRP):
                                pe.wait_ge(s["pc"], now(g, lvl, 6))
                                pe.wait_ge(s["xf"], now(g, lvl, 6))
                                for n, h in enumerate(heads(g)):
                                    ins = nc.tensor.matmul(bank[2 + 4 * g][:, n * nn:n * nn + nn], Xin[:, h, :], Pin[:, h, :],
                                                           start=True, stop=True)
                                ins.then_inc(s["q"], 1)
                                if size == 32:
                                    pe.wait_ge(s["dd"], now(g))
                                    pe.wait_ge(s["eqx"], now(g))
                                    for n, h in enumerate(heads(g)):
                                        ins = nc.tensor.matmul(bank[3 + 4 * g][:, n * P:n * P + P], PF[:, h, :], XF[:, h, :],
                                                               start=True, stop=True)
                                    ins.then_inc(s["r"], 1)
                        for g in range(GRP):
                            pe.wait_ge(s["kbe"], now(g))
                            pe.wait_ge(s["yc"], now(g, 6, 7))
                            pe.wait_ge(s["at2"], now(g))
                            for n, h in enumerate(heads(g)):
                                ins = nc.tensor.matmul(bank[1 + 4 * g][:, n * P:n * P + P], kbe[:, h, :], Y2[:, h, :],
                                                       start=True, stop=True)
                            ins.then_inc(s["w"], 1)
                        for g in range(GRP):
                            pe.wait_ge(s["nw"], now(g))
                            for n, h in enumerate(heads(g)):
                                here = bank[4 * g][:, n * P:n * P + P]
                                nc.tensor.matmul(here, Y2[:, h, :], vb[:, h, :], start=True, stop=False)
                                ins = nc.tensor.matmul(here, nw[:, h, :], state[:, h, :], start=False, stop=True)
                            ins.then_inc(s["uv"], 1)
                        for g in range(GRP):
                            pe.wait_ge(s["vn"], now(g) + 2)
                            pe.wait_ge(s["qe"], now(g))
                            for n, h in enumerate(heads(g)):
                                here = bank[2 + 4 * g][:, n * P:n * P + P]
                                nc.tensor.matmul(here, qe[:, h, :], state[:, h, :], start=True, stop=False)
                                ins = nc.tensor.matmul(here, at[:, h, :], vn[:, h, :], start=False, stop=True)
                            ins.then_inc(s["o"], 1)
                            pe.wait_ge(s["kdec"], now(g))
                            for n, h in enumerate(heads(g)):
                                ins = nc.tensor.matmul(bank[3 + 4 * g][:, n * P:n * P + P], kdec[:, h, :], vn[:, h, :],
                                                       start=True, stop=True)
                            ins.then_inc(s["kv"], 1)
                for n, v in (("vn", 2), ("state", 2), ("on", 2), ("y", 4)):
                    pe.sem_inc(s[n], v)
                pe.wait_ge(s["pre_dve"], 24)
                pe.wait_ge(s["pre_act"], 8)
                body(0, None)
                with pe.Fori(0, NB // 2 - 1) as i:
                    body(i + 1, i)
                turn_out(NB - 1)

            @block.scalar
            def _(act):
                st = Steps(act, s["pre_act"])
                act.wait_ge(s["pre_dve"], 1)
                act.wait_ge(s["consts"], 48)
                st.done(nc.scalar.activation(small[:, 0:2, :].rearrange("p a b -> p (a b)"), core.dn_sums[:, :], ACT.Sqrt,
                                             bias=eps4[:, 0:1]))
                ab = core.dn_ab[:, :].rearrange("p (b k h) -> p b k h", b=NB, k=2)
                st.done(nc.scalar.activation(small[:, 2, :].rearrange("p (b h) -> p b h", b=NB), ab[:, :, 0, :], ACT.Tanh,
                                             scale=0.5))
                act.wait_ge(s["pre_dve"], 4)
                st.done(nc.scalar.activation(small[:, 4, :], small[:, 4, :], ACT.Exp, scale=-1.0))
                act.wait_ge(s["pre_dve"], 5)
                st.done(nc.scalar.activation(small[:, 6, :], small[:, 5, :], ACT.Ln))
                st.done(nc.scalar.activation(head_v[:, 0, :], head_v[:, 0, :], ACT.Exp))
                act.wait_ge(s["pre_dve"], 18)

                def flat(k):
                    return sA[:, k, :, :].rearrange("p b h -> p (b h)")
                st.done(nc.scalar.activation(small[:, 0, :], flat(GC), ACT.Exp))
                act.wait_ge(s["pre_pe"], 2)
                st.done(nc.scalar.activation(flat(EGL), bank[1][:, 0:64], ACT.Exp))
                st.done(nc.scalar.activation(flat(EDEC), small[:, 1, :], ACT.Exp))

                def body(it, last):
                    for bb in range(2):
                        def now(g, lvl=None, per=1):
                            return it * (4 * per) + (bb * 2 * per + (lvl or 0) * 2 + g + 1)
                        for g in range(GRP):
                            act.wait_ge(s["knt"], now(g))
                            nc.scalar.activation(grp(knT, g), bk(2, g), ACT.Copy).then_inc(s["kntc"], 1)
                        for g in range(GRP):
                            act.wait_ge(s["e0"], now(g))
                            nc.scalar.activation(grp(e0, g), grp(e0, g), ACT.Exp, scale=-1.0).then_inc(s["e0x"], 1)
                            act.wait_ge(s["e1"], now(g))
                            nc.scalar.activation(grp(e1, g), grp(e1, g), ACT.Exp).then_inc(s["e1x"], 1)
                            nc.scalar.activation(grp(eq, g), bk(3, g), ACT.Exp).then_inc(s["eqx"], 1)
                        for lvl, size in enumerate(LEVELS):
                            full = size >= 32
                            for g in range(GRP):
                                act.wait_ge(s["p"], now(g, lvl, 6))
                                src = bk(0, g) if full else bk(0, g, P)
                                nc.scalar.activation(grp(PF if full else Pc, g), src, ACT.Copy).then_inc(s["pc"], 1)
                        for g in range(GRP):
                            act.wait_ge(s["w"], now(g))
                            nc.scalar.activation(grp(nw, g), bk(1, g), ACT.Copy, scale=-1.0).then_inc(s["nw"], 1)
                        for g in range(GRP):
                            act.wait_ge(s["o"], now(g))
                            nc.scalar.activation(grp(sqo, g), bk(2, g), ACT.Square).then_inc(s["sqo"], 1)
                        act.wait_ge(s["var"], it * 2 + (bb + 1))
                        nc.scalar.activation(tiny[:, 1, :], tiny[:, 0, :], ACT.Sqrt, bias=core.eps[:, 0:1]).then_inc(s["std"], 1)
                with act.Fori(0, NB // 2) as it:
                    body(it, False)

            @block.gpsimd
            def _(pool):
                nc.gpsimd.memset(XF[:, :, :], 0.0).then_inc(s["zeroed"], 1)
                nc.gpsimd.memset(YF[:, :, :], 0.0).then_inc(s["zeroed"], 1)
                pool.wait_ge(s["consts"], 48)

                def body(it, last):
                    for bb in range(2):
                        def now(g, lvl=None, per=1):
                            return it * (4 * per) + (bb * 2 * per + (lvl or 0) * 2 + g + 1)
                        pool.wait_ge(s["cur"], it * 2 + (bb + 1))
                        for g in range(GRP):
                            gs = slice(4 * g, 4 * g + 4)
                            nc.gpsimd.tensor_tensor(grp(gu, g), bcast_mid(upper, 4), bcast_last(cur[:, G, gs], P), ALU.mult)\
                                .then_inc(s["gu"], 1)
                        for g in range(GRP):
                            gs = slice(4 * g, 4 * g + 4)
                            pool.wait_ge(s["e0x"], now(g))
                            nc.gpsimd.tensor_tensor(grp(e0, g), grp(e0, g), bcast_last(cur[:, BETA, gs], P), ALU.mult)\
                                .then_inc(s["m0"], 1)
                        for lvl, size in enumerate(LEVELS):
                            for g in range(GRP):
                                if lvl == 0:
                                    pool.wait_ge(s["A"], now(g))
                                nc.gpsimd.tensor_tensor(grp(AL[size], g), grp(Am, g), bcast_mid(level_mask[size], 4), ALU.mult)\
                                    .then_inc(s["al"], 1)
                            if lvl == 1:
                                for g in range(GRP):
                                    pool.wait_ge(s["e1x"], now(g))
                                    nc.gpsimd.tensor_tensor(grp(e1, g), grp(e1, g), bcast_mid(upper, 4), ALU.mult)\
                                        .then_inc(s["m1"], 1)
                        for g in range(GRP):
                            gs = slice(4 * g, 4 * g + 4)
                            nc.gpsimd.tensor_tensor(grp(kbe, g), grp(kn, g), bcast_last(cur[:, KBES, gs], P), ALU.mult)\
                                .then_inc(s["kbe"], 1)
                            nc.gpsimd.tensor_tensor(grp(kdec, g), grp(kn, g), bcast_last(cur[:, EDEC, gs], P), ALU.mult)\
                                .then_inc(s["kdec"], 1)
                            pool.wait_ge(s["eqx"], now(g))
                            nc.gpsimd.tensor_tensor(grp(qe, g), grp(qT[bb], g), grp(eq, g), ALU.mult).then_inc(s["qe"], 1)
                            pool.wait_ge(s["state"], now(g))
                            nc.gpsimd.tensor_tensor(grp(Sd, g), grp(state, g), bcast_last(cur[:, EGL, gs], P), ALU.mult)\
                                .then_inc(s["sd"], 1)
                with pool.Fori(0, NB // 2) as it:
                    body(it, False)

            @block.vector
            def _(dve):
                st = Steps(dve, s["pre_dve"])
                V = nc.vector

                def flat(k):
                    return sA[:, k, :, :].rearrange("p b h -> p (b h)")

                def by_head(ap):
                    return bcast_mid(ap, NB)
                ab = core.dn_ab[:, :].rearrange("p (b k h) -> p b k h", b=NB, k=2)
                st.done(V.memset(eps4[:, :], 4 * EPS))
                dve.wait_ge(s["pre_act"], 1)
                st.done(V.reciprocal(small[:, 0:2, :].rearrange("p a b -> p (a b)"),
                                     small[:, 0:2, :].rearrange("p a b -> p (a b)")))
                dve.wait_ge(s["consts"], 48)
                x3 = small[:, 3, :]
                st.done(V.tensor_tensor(x3.rearrange("p (b h) -> p b h", b=NB), ab[:, :, 1, :], by_head(head_v[:, 1, :]),
                                        ALU.add))
                st.done(V.scalar_tensor_tensor(small[:, 4, :], x3, -1.0, x3, op0=ALU.mult, op1=ALU.max))
                dve.wait_ge(s["pre_act"], 3)
                e, w1, ln = small[:, 4, :], small[:, 5, :], small[:, 6, :]
                st.done(V.tensor_scalar(w1, e, 1.0, None, op0=ALU.add))
                dve.wait_ge(s["pre_act"], 5)
                fix = small[:, 7, :]
                st.done(V.tensor_scalar(fix, w1, -1.0, None, op0=ALU.add))
                st.done(V.tensor_tensor(fix, e, fix, ALU.subtract))
                st.done(V.reciprocal(w1, w1))
                st.done(V.tensor_tensor(fix, fix, w1, ALU.mult))
                st.done(V.tensor_tensor(ln, ln, fix, ALU.add))
                st.done(V.scalar_tensor_tensor(ln, x3, 0.0, ln, op0=ALU.max, op1=ALU.add))
                st.done(V.tensor_tensor(w1.rearrange("p (b h) -> p b h", b=NB), ln.rearrange("p (b h) -> p b h", b=NB),
                                        by_head(head_v[:, 0, :]), ALU.mult))
                st.done(V.tensor_scalar(w1, w1, -1.0, None, op0=ALU.mult))
                st.done(V.tensor_copy(flat(G), w1))
                dve.wait_ge(s["pre_pe"], 2)
                st.done(V.tensor_scalar(flat(RK), small[:, 1, :], 1.0, None, op0=ALU.mult))
                st.done(V.tensor_copy(flat(GC), bank[0][:, 0:64]))
                st.done(V.tensor_scalar(flat(RQS), small[:, 0, :], float(P) ** -0.5, None, op0=ALU.mult))
                st.done(V.tensor_tensor(small[:, 1, :], bank[1][:, 0:64], flat(GC), ALU.subtract))
                st.done(V.tensor_tensor(flat(S2), flat(RQS), flat(RQS), ALU.mult))
                st.done(V.tensor_scalar(flat(S2), flat(S2), 1.0 / P, None, op0=ALU.mult))
                st.done(V.tensor_scalar(flat(BETA), small[:, 2, :], 0.5, 0.5, op0=ALU.mult, op1=ALU.add))
                st.done(V.tensor_scalar(flat(VBS), flat(BETA), 0.5, None, op0=ALU.mult))
                dve.wait_ge(s["pre_act"], 8)
                st.done(V.tensor_tensor(flat(KBES), flat(BETA), small[:, 0, :], ALU.mult))
                st.done(V.tensor_scalar(nwcol[:, :], core.col1[:, core.r1["dn_norm"]:core.r1["dn_norm"] + 1], 0.5, None,
                                        op0=ALU.mult))
                dve.wait_ge(s["zeroed"], 2)

                def quads(dst, src, g, transposed, signal=None):
                    for a in range(4):
                        rows = slice(32 * a, 32 * a + 32)
                        to = dst[rows, 4 * g:4 * g + 4, 32 * a:32 * a + 32]
                        if transposed:
                            ins = V.transpose(to, src[rows, 4 * g:4 * g + 4, :])
                        else:
                            ins = V.tensor_copy(to, src[rows, 4 * g:4 * g + 4, :])
                    return ins

                def out(it, bb):
                    for g in range(GRP):
                        dve.wait_ge(s["ot"], it * 4 + (bb * 2 + g + 1))
                        V.scalar_tensor_tensor(y[:, 4 * g:4 * g + 4, bass.ds(it * 256 + bb * P, P)], bk(1, g),
                                               nwcol[:, 0:1], grp(zT[bb], g), op0=ALU.mult, op1=ALU.mult)\
                            .then_inc(s["y"], 1)

                def body(it, previous):
                    for bb in range(2):
                        def now(g, lvl=None, per=1):
                            return it * (4 * per) + (bb * 2 * per + (lvl or 0) * 2 + g + 1)
                        once = it * 2 + (bb + 1)
                        V.tensor_copy(cur[:, :, :], sA[:, :, it * 2 + bb, :]).then_inc(s["cur"], 1)
                        dve.wait_ge(s["cur"], once)
                        for g in range(GRP):
                            gs = slice(4 * g, 4 * g + 4)
                            dve.wait_ge(s["kt"], now(g))
                            V.tensor_tensor(grp(kn, g), bk(0, g), bcast_last(cur[:, RK, gs], P), ALU.mult).then_inc(s["kn"], 1)
                        if bb:
                            out(it, 0)
                        elif previous is not None:
                            out(previous, 1)
                        for g in range(GRP):
                            gs = slice(4 * g, 4 * g + 4)
                            dve.wait_ge(s["vt"], now(g))
                            V.tensor_tensor(grp(vb, g), bk(1, g), bcast_last(cur[:, VBS, gs], P), ALU.mult).then_inc(s["vb"], 1)
                        for g in range(GRP):
                            gs = slice(4 * g, 4 * g + 4)
                            dve.wait_ge(s["bc"], now(g))
                            V.tensor_tensor(grp(e1, g), bk(3, g), bcast_last(cur[:, GC, gs], P), ALU.subtract)\
                                .then_inc(s["dd"], 1)
                            dve.wait_ge(s["dd"], now(g))
                            V.tensor_scalar(grp(e0, g), grp(e1, g), 0.0, None, op0=ALU.max).then_inc(s["e0"], 1)
                            dve.wait_ge(s["e0"], now(g))
                            V.tensor_scalar(grp(e1, g), grp(e1, g), 0.0, None, op0=ALU.min).then_inc(s["e1"], 1)
                        for g in range(GRP):
                            dve.wait_ge(s["g"], now(g))
                            dve.wait_ge(s["m0"], now(g))
                            V.tensor_tensor(grp(Am, g), bk(0, g), grp(e0, g), ALU.mult).then_inc(s["A"], 1)
                            dve.wait_ge(s["A"], now(g))
                            for a in range(4):
                                rows = slice(32 * a, 32 * a + 32)
                                ins = V.tensor_copy(Xc[rows, 4 * g:4 * g + 4, :], Am[rows, 4 * g:4 * g + 4, 32 * a:32 * a + 32])
                            ins.then_inc(s["compact"], 1)
                            dve.wait_ge(s["compact"], now(g))
                            V.tensor_tensor(grp(Xc, g), grp(Xc, g), bcast_mid(mask1_c, 4), ALU.mult).then_inc(s["x1"], 1)
                            dve.wait_ge(s["x1"], it * 8 + (bb * 4 + 2 * g + 1))
                            V.tensor_tensor(grp(Xc, g), bcast_mid(ident_c, 4), grp(Xc, g), ALU.subtract).then_inc(s["x1"], 1)
                            dve.wait_ge(s["x1"], it * 8 + (bb * 4 + 2 * g + 2))
                            V.transpose(grp(Yc, g), grp(Xc, g)).then_inc(s["yc"], 1)
                            quads(XF, Xc, g, False).then_inc(s["xf"], 1)
                        for lvl, size in enumerate(LEVELS):
                            full = size >= 32
                            for g in range(GRP):
                                dve.wait_ge(s["q"], now(g, lvl, 6))
                                if not full:
                                    V.tensor_tensor(grp(Yc, g), grp(Yc, g), bk(2, g, P), ALU.subtract).then_inc(s["yc" if size < 16 else "y16"], 1)
                                    if size < 16:
                                        dve.wait_ge(s["yc"], now(g, lvl + 1, 7))
                                    else:
                                        dve.wait_ge(s["y16"], now(g))
                                    quads(XF, Yc, g, True).then_inc(s["xf"], 1)
                                    if size == 16:
                                        quads(YF, Yc, g, False).then_inc(s["yc"], 1)
                                elif size == 32:
                                    V.tensor_tensor(grp(Y2, g), grp(YF, g), bk(2, g), ALU.subtract).then_inc(s["yc"], 1)
                                    dve.wait_ge(s["r"], now(g))
                                    V.tensor_tensor(grp(X2, g), grp(XF, g), bk(3, g), ALU.subtract).then_inc(s["xf"], 1)
                                else:
                                    V.tensor_tensor(grp(Y2, g), grp(Y2, g), bk(2, g), ALU.subtract).then_inc(s["yc"], 1)
                            if lvl == 1:
                                for g in range(GRP):
                                    dve.wait_ge(s["at"], now(g))
                                    dve.wait_ge(s["m1"], now(g))
                                    V.tensor_tensor(grp(at, g), bk(1, g), grp(e1, g), ALU.mult).then_inc(s["at2"], 1)
                        for g in range(GRP):
                            dve.wait_ge(s["uv"], now(g))
                            V.tensor_copy(grp(vn, g), bk(0, g)).then_inc(s["vn"], 1)
                        for g in range(GRP):
                            dve.wait_ge(s["kv"], now(g))
                            dve.wait_ge(s["sd"], now(g))
                            V.tensor_tensor(grp(state, g), grp(Sd, g), bk(3, g), ALU.add).then_inc(s["state"], 1)
                        for g in range(GRP):
                            dve.wait_ge(s["sqo"], now(g))
                            V.tensor_reduce(tiny[:, 0, 4 * g:4 * g + 4], grp(sqo, g), AX_X, ALU.add).then_inc(s["sqr"], 1)
                        dve.wait_ge(s["sqr"], now(1))
                        V.tensor_tensor(tiny[:, 0, :], tiny[:, 0, :], cur[:, S2, :], ALU.mult).then_inc(s["var"], 1)
                        dve.wait_ge(s["std"], once)
                        V.reciprocal(tiny[:, 2, :], tiny[:, 1, :]).then_inc(s["rec"], 1)
                        dve.wait_ge(s["rec"], once)
                        V.tensor_tensor(tiny[:, 3, :], tiny[:, 2, :], cur[:, RQS, :], ALU.mult).then_inc(s["f"], 1)
                        dve.wait_ge(s["f"], once)
                        for g in range(GRP):
                            gs = slice(4 * g, 4 * g + 4)
                            V.tensor_tensor(grp(on, g), bk(2, g), bcast_last(tiny[:, 3, gs], P), ALU.mult).then_inc(s["on"], 1)
                body(0, None)
                with dve.Fori(0, NB // 2 - 1) as i:
                    body(i + 1, i)
                out(NB // 2 - 1, 1)


WINDOWS = (2, 4, 8, 16)
NG = len(WINDOWS)
GT = KT // NG
HALO = 16


def pool_phase(core, A, half):
    core.begin_phase()
    nc = core.nc
    tag = f"pool{half}"
    T = S = 2 * GT
    h_hi, h_lo, y, col1, r1 = core.h_hi, core.h_lo, core.y, core.col1, core.r1
    w_in = A["pool_w_in"][0]
    group_v = A["pool_group_w"][0].rearrange("g (k p) o -> p g k o", p=P)
    with ExitStack() as ctx:
        w = Weights(core, ctx, tag, S)

        def two(name, width=CH):
            return [core.sb(f"{tag}_{name}{i}", [P, width], F32, ctx) for i in range(GT)]
        u = two("u", HALO + CH)
        sums = [core.sb(f"{tag}_sums{i}", [P, HALO + CH], F32, ctx) for i in range(2)]
        p = two("p")
        sil = two("silu")
        pg = core.sb(f"{tag}_grouped", [P, CH], F32, ctx)
        gw = core.sb(f"{tag}_group_w", [P, GT, GT * P], F32, ctx)
        recip = core.sb(f"{tag}_recip", [P, NG, HALO], F32, ctx)
        s_rc = core.sem(f"{tag}_recip_loaded")
        s_gw = core.sem(f"{tag}_group_w_loaded")
        s_head = core.sem(f"{tag}_halo_ready")
        s_u = core.sem(f"{tag}_u_copied")
        s_p = core.sem(f"{tag}_p_ready")
        s_o = core.sem(f"{tag}_group_multiplied")
        s_th = core.sem(f"{tag}_tanh_ready")
        s_y = core.sem(f"{tag}_y_ready")
        s_dve = core.sem(f"{tag}_dve")

        with nc.Block() as block:
            @block.sync
            def _(sp):
                core.clear_last_phase(sp)
                sp.dma_start(recip[:, :, :], A["pool_recip"]).then_inc(s_rc, 16)
                with sp.Fori(0, NG) as g:
                    for t in range(T):
                        w.load(sp, wtile(w_in, bass.ds(g * (GT * P) + (t // GT * D + t % GT * P), P)), t, g * T)
                        if t == 1:
                            sp.wait_ge(s_o, g * NCH + NCH)
                            sp.dma_start(gw[:, :, :], group_v[:, g, :, :]).then_inc(s_gw, 16)

            @block.gpsimd
            def _(pool):
                pool.sem_inc(w.split, 2)
                with pool.Fori(0, NG) as g:
                    for t in range(T):
                        w.subtract(pool, t, g * T)

            @block.tensor
            def _(pe):
                pe.sem_inc(w.projected, 2 * S)
                pe.sem_inc(s_o, NCH)
                pe.sem_inc(s_y, GT)
                pe.sem_inc(s_u, GT)
                with pe.Fori(0, NG) as g:
                    for c in range(NCH):
                        for t in range(T):
                            if t < GT:
                                pe.wait_ge(s_u, g * (NCH * GT) + (c * GT + t + 1))
                            else:
                                pe.wait_ge(s_y, g * (NCH * GT) + (c * GT + t - GT + 1))
                            w.multiply(pe, core.bank[t][:, :], t, h_hi, h_lo, slice(c * CH, c * CH + CH), g * T)
                        if c == 0:
                            pe.wait_ge(s_gw, g * 16 + 16)
                        pe.wait_ge(s_p, g * (NCH * GT) + (c * GT + GT))
                        for o in range(GT):
                            for k in range(GT):
                                ins = nc.tensor.matmul(core.bank[T + o][:, :], gw[:, k, o * P:o * P + P], p[k][:, :],
                                                       start=(k == 0), stop=(k == GT - 1))
                        ins.then_inc(s_o, 1)

            @block.scalar
            def _(act):
                for t in range(T):
                    w.round(act, t, T + t + 1)

                def body(g, last):
                    for c in range(NCH):
                        for t in range(T):
                            act.wait_ge(w.projected, g * (NCH * T) + (2 * S + c * T + t + 1))
                            if t < GT:
                                act.wait_ge(s_head, g * (NCH * GT) + (c * GT + t + 1))
                                nc.scalar.activation(u[t][:, HALO:HALO + CH], core.bank[t][:, :], ACT.Copy)\
                                    .then_inc(s_u, 1)
                            else:
                                act.wait_ge(s_y, g * (NCH * GT) + (c * GT + t - GT + 1))
                                nc.scalar.activation(sil[t - GT][:, :], core.bank[t][:, :], ACT.Tanh, scale=0.5)\
                                    .then_inc(s_th, 1)
                            if c == 1 and not last:
                                w.round(act, t, g * (NCH * T) + (NCH * T + T + t + 1), arrivals=g * (8 * T) + 8 * T)
                each(act, NG, body)

            @block.vector
            def _(dve):
                V = nc.vector
                st = Steps(dve, s_dve)
                for t in range(GT):
                    V.tensor_copy(u[t][:, 0:HALO], core.pool_halo[:, t, :]).then_inc(s_head, 1)
                dve.wait_ge(s_rc, 16)
                for g, win in enumerate(WINDOWS):
                    for c in range(NCH):
                        unit = g * NCH + c
                        for t in range(GT):
                            n = unit * GT + t
                            dve.wait_ge(s_u, n + GT + 1)
                            src, span = u[t], 1
                            while span < win:
                                dst = sums[span.bit_length() % 2]
                                first = 2 * span - 1
                                st.done(V.tensor_tensor(dst[:, first:HALO + CH], src[:, first:HALO + CH],
                                                        src[:, first - span:HALO + CH - span], ALU.add))
                                src, span = dst, 2 * span
                            if n >= GT:
                                dve.wait_ge(s_o, unit + NCH)
                            ins = V.scalar_tensor_tensor(p[t][:, :], src[:, HALO:HALO + CH], 1.0 / win,
                                                         u[t][:, HALO:HALO + CH], op0=ALU.mult, op1=ALU.subtract)
                            if half == 0 and c == 0:
                                st.done(ins)
                                st.done(V.tensor_tensor(src[:, HALO:2 * HALO], src[:, HALO:2 * HALO], recip[:, g, :],
                                                        ALU.mult))
                                ins = V.tensor_tensor(p[t][:, 0:HALO], src[:, HALO:2 * HALO], u[t][:, HALO:2 * HALO],
                                                      ALU.subtract)
                            ins.then_inc(s_p, 1)
                            dve.wait_ge(s_p, n + 1)
                            tail = u[t][:, CH:CH + HALO]
                            if c == NCH - 1:
                                st.done(V.tensor_copy(core.pool_halo[:, g * GT + t, :], tail))
                                tail = core.pool_halo[:, g * GT + GT + t, :] if g < NG - 1 else None
                            if tail is not None:
                                V.tensor_copy(u[t][:, 0:HALO], tail).then_inc(s_head, 1)
                        for o in range(GT):
                            n, d = unit * GT + o, g * GT + o
                            dve.wait_ge(s_th, n + 1)
                            st.done(V.scalar_tensor_tensor(sil[o][:, :], sil[o][:, :], 1.0, core.bank[GT + o][:, :],
                                                           op0=ALU.add, op1=ALU.mult))
                            dve.wait_ge(s_o, unit + NCH + 1)
                            st.done(V.tensor_scalar(pg[:, :], core.bank[T + o][:, :],
                                                    col1[:, r1["pool_b"] + d:r1["pool_b"] + d + 1],
                                                    col1[:, r1["pool_scale"] + d:r1["pool_scale"] + d + 1],
                                                    op0=ALU.add, op1=ALU.mult))
                            V.scalar_tensor_tensor(y[:, d, c * CH:c * CH + CH], pg[:, :], 0.5, sil[o][:, :],
                                                   op0=ALU.mult, op1=ALU.mult).then_inc(s_y, 1)
                            dve.wait_ge(s_y, n + GT + 1)


HQ, HD, QW = 16, 64, 64
KVH = 2
NW = CH // QW
REL = 192
MASKED = -1e30


def swa_phase(core, A, half):
    core.begin_phase()
    nc = core.nc
    tag = f"swa{half}"
    T = S = 2
    h_hi, h_lo, y = core.h_hi, core.h_lo, core.y
    w_in = A["swa_w_in"][0]
    QD, KD = HQ * HD, KVH * HD
    bias_at = core.r1["swa_b"]
    bank = core.bank
    with ExitStack() as ctx:
        w = Weights(core, ctx, tag, S)
        qs = core.sb(f"{tag}_q", [P, CH], F32, ctx)
        kk = [core.sb(f"{tag}_keys{i}", [P, QW + HALF], F32, ctx) for i in range(KVH)]
        vals = core.sb(f"{tag}_values", [P, HALF // P + 1, KD], F32, ctx)
        vals_even = core.sb(f"{tag}_values_even", [P, HALF // P, KD], F32, ctx)
        vbias = core.sb(f"{tag}_value_bias", [P, KD], F32, ctx)
        lg = [core.sb(f"{tag}_probs{i}", [P, NW, 2 * QW], F32, ctx) for i in range(2)]
        sil = [core.sb(f"{tag}_silu{i}", [P, CH], F32, ctx) for i in range(2)]
        relb = core.sb(f"{tag}_rel_bias", [P, KT, 2 * QW], F32, ctx)
        sink = core.sb(f"{tag}_sinks", [P, HQ], F32, ctx)
        par = core.sb(f"{tag}_params", [P, KT, 4], F32, ctx)
        cur = core.sb(f"{tag}_cur", [P, 4], F32, ctx)
        tiny = core.sb(f"{tag}_tiny", [P, 4, NW], F32, ctx)
        if half == 0:
            onehot = core.sb(f"{tag}_onehot", [32, REL], F32, ctx)
            rb = core.sb(f"{tag}_rb", [32, HQ], F32, ctx)
            tab = core.sb(f"{tag}_table", [HQ, REL], F32, ctx)
            s_rb = core.sem(f"{tag}_rb_loaded")
            s_tp = core.sem(f"{tag}_table_multiplied")
            s_tc = core.sem(f"{tag}_table_copied")
            s_tw = core.sem(f"{tag}_table_stored")
        names = ("vectors", "bias", "keys", "keys_doubled", "values", "carried", "par", "cur", "q", "qk",
                 "logits", "max", "shifted", "exp", "den", "sinkexp", "rec", "probs", "probs_t", "copied", "pv", "y",
                 "tanh", "g1", "g2", "masked")
        s = {n: core.sem(f"{tag}_{n}") for n in names}
        table = core.swa_table

        def skewed(b):
            return bass.AP(tensor=table.tensor, offset=table.offset + b * QW * REL + QW - 1,
                           ap=[[REL - 1, QW], [2 * QW * REL, KT], [1, 2 * QW]])

        with nc.Block() as block:
            @block.sync
            def _(sp):
                core.clear_last_phase(sp)
                w.load(sp, wtile(w_in, slice(QD, QD + KD)), 0)
                w.load(sp, wtile(w_in, slice(QD + KD, QD + 2 * KD)), 1)
                sp.dma_start(sink[:, :], A["swa_sinks"].partition_broadcast(P)[:, 0, :]).then_inc(s["vectors"], 16)
                vb = A["swa_b_in"][:, QD + KD:QD + 2 * KD]
                sp.dma_start(vbias[:, :], vb.partition_broadcast(P)[:, 0, :]).then_inc(s["vectors"], 16)
                if half == 0:
                    sp.dma_start(onehot[:, :], A["rel_onehot"]).then_inc(s_rb, 16)
                    sp.dma_start(rb[:, :], A["rel_bias"]).then_inc(s_rb, 16)
                    sp.wait_ge(s_tc, 1)
                    src = tab[:, :].unsqueeze(1).broadcast_to([HQ, QW, REL])
                    sp.dma_start(table, src).then_inc(s_tw, 16)
                    sp.wait_ge(s_tw, 16)
                for b in range(2):
                    sp.dma_start(relb[b * QW:b * QW + QW, :, :], skewed(b)).then_inc(s["bias"], 16)
                sp.wait_ge(s["keys"], 4)
                sp.dma_start(kk[0][QW:P, QW:QW + HALF], kk[0][0:QW, QW:QW + HALF]).then_inc(s["keys_doubled"], 16)
                sp.dma_start(kk[1][0:QW, QW:QW + HALF], kk[1][QW:P, QW:QW + HALF]).then_inc(s["keys_doubled"], 16)
                with sp.Fori(0, KT) as n:
                    for t in range(T):
                        w.load(sp, wtile(w_in, bass.ds(n * P + t * (QD + 2 * KD), P)), t, n * T + T)

            @block.gpsimd
            def _(pool):
                pool.sem_inc(w.split, 2)
                for t in range(2 * T):
                    w.subtract(pool, t % T, t // T * T)

                def body(n, last):
                    for c in range(NCH):
                        unit = n * NCH + (c + 1)
                        pool.wait_ge(s["rec"], unit)
                        nc.gpsimd.tensor_tensor(lg[c][:, :, :], lg[c][:, :, :], bcast_last(tiny[:, 3, :], 2 * QW), ALU.mult)\
                            .then_inc(s["probs"], 1)
                        if not last:
                            w.subtract(pool, c, n * T + 2 * T)
                each(pool, KT, body)

            @block.tensor
            def _(pe):
                pe.sem_inc(w.projected, 2 * S)
                if half == 0:
                    pe.wait_ge(s_rb, 32)
                    nc.tensor.matmul(bank[5][0:HQ, 0:REL], rb[:, :], onehot[:, :], start=True, stop=True).then_inc(s_tp, 1)
                for c in range(NCH):
                    w.multiply(pe, bank[c][:, :], 0, h_hi, h_lo, slice(c * CH, c * CH + CH))
                pe.wait_ge(w.split, 4)
                for b in range(HALF // P):
                    for k in range(KT):
                        for m, (x, ww) in enumerate(((h_hi, w.hi), (h_hi, w.lo), (h_lo, w.hi))):
                            ins = nc.tensor.matmul(bank[3 + b // 4][:, b % 4 * P:b % 4 * P + P], x[:, k, b * P:b * P + P],
                                                   ww[1][:, k, :], start=(k == 0 and m == 0), stop=(k == KT - 1 and m == 2))
                    if b % 4 == 3:
                        ins.then_inc(w.projected, 1)

                def logits(kv, c):
                    for j in range(NW):
                        at = (c * NW + j) * QW
                        for b in range(2):
                            rows = slice(b * HD, b * HD + HD)
                            q = qs[rows, j * QW:j * QW + QW]
                            out = bank[3 + j // 4][rows, j % 4 * P:j % 4 * P + P]
                            if j % 2:
                                ins = nc.tensor.matmul(out, q, kk[kv][rows, at:at + 2 * QW], start=True, stop=True)
                            else:
                                nc.tensor.matmul(out[:, 0:QW], q, kk[kv][rows, at + QW:at + 2 * QW], start=True, stop=True)
                                ins = nc.tensor.matmul(out[:, QW:P], q, kk[kv][rows, at:at + QW], start=True, stop=True)
                    ins.then_inc(s["qk"], 1)

                def turn(unit, c, final=False):
                    pe.wait_ge(s["probs"], unit)
                    for j in range(NW):
                        if j == NW - 1 and not final:
                            pe.wait_ge(s["q"], unit + 1)
                        ins = nc.tensor.transpose(bank[5 + j // 4][:, j % 4 * P:j % 4 * P + P], lg[c][:, j, :], core.ident[:, :])
                    ins.then_inc(s["probs_t"], 1)

                def weigh_waits(unit):
                    return (s["copied"], unit), (s["y"], unit + 1)

                def weigh(kv, c):
                    for j in range(NW):
                        tile = (c * NW + j + 1) // 2
                        for b in range(2):
                            out = bank[7][b * HD:b * HD + HD, j * QW:j * QW + QW]
                            v = (vals if j % 2 else vals_even)[:, :, kv * HD:kv * HD + HD]
                            pr = lg[c][:, j, b * QW:b * QW + QW]
                            ins = nc.tensor.matmul(out, v[:, tile, :], pr, start=True, stop=True)
                    ins.then_inc(s["pv"], 1)

                def body(n, kv, prev_kv):
                    for c in range(NCH):
                        cols = slice(c * CH, c * CH + CH)
                        before = c > 0 or prev_kv is not None
                        w.multiply(pe, bank[0][:, :], 0, h_hi, h_lo, cols, n * T + T)
                        if before:
                            turn(n * NCH + c, (c + 1) % NCH)
                        else:
                            pe.wait_ge(s["q"], 1)
                        logits(kv, c)
                        w.multiply(pe, bank[1 + c][:, :], 1, h_hi, h_lo, cols, n * T + T,
                                   weigh_waits(n * NCH + c) if before else ())
                        if before:
                            weigh(kv if c else prev_kv, (c + 1) % NCH)

                pe.wait_ge(s["keys"], 4)
                pe.wait_ge(s["keys_doubled"], 32)
                pe.wait_ge(s["carried"], 3)
                pe.wait_ge(s["values"], 4)
                per = KT // KVH
                for kv in range(KVH):
                    body(kv * per, kv, kv - 1 if kv else None)
                    with pe.Fori(0, per - 1) as i:
                        body(i + (kv * per + 1), kv, kv)
                turn(KT * NCH, NCH - 1, final=True)
                for sem, value in weigh_waits(KT * NCH):
                    pe.wait_ge(sem, value)
                weigh(KVH - 1, NCH - 1)

            @block.scalar
            def _(act):
                for t in range(T):
                    w.round(act, t, T + t + 1)
                if half == 0:
                    act.wait_ge(s_tp, 1)
                    nc.scalar.activation(tab[:, :], bank[5][0:HQ, 0:REL], ACT.Copy).then_inc(s_tc, 1)
                kbias = core.col1[:, bias_at + KT:bias_at + KT + 1]
                for c in range(NCH):
                    act.wait_ge(w.projected, 2 * S + c + 1)
                    cols = slice(QW + c * CH, QW + c * CH + CH)
                    for i in range(KVH):
                        rows = slice(i * HD, i * HD + HD)
                        nc.scalar.activation(kk[i][rows, cols], bank[c][rows, :], ACT.Identity, bias=kbias[rows, :])\
                            .then_inc(s["keys"], 1)
                for t in range(T):
                    w.round(act, t, 2 * T + T + t + 1, arrivals=8 * T)

                def transposed(unit, c):
                    act.wait_ge(s["probs_t"], unit)
                    for g in range(2):
                        ins = nc.scalar.activation(lg[c][:, 4 * g:4 * g + 4, :].rearrange("p j k -> p (j k)"), bank[5 + g][:, :],
                                                   ACT.Copy)
                    ins.then_inc(s["copied"], 1)

                def body(n, last, before):
                    for c in range(NCH):
                        unit = n * NCH + (c + 1)
                        act.wait_ge(w.projected, n * (NCH * T) + (2 * S + 4 + c * T + 1))
                        act.wait_ge(s["cur"], n + 1)
                        nc.scalar.activation(qs[:, :], bank[0][:, :], ACT.Identity, scale=HD ** -0.5, bias=cur[:, 0:1])\
                            .then_inc(s["q"], 1)
                        if c == 1 and not last:
                            w.round(act, 0, n * (NCH * T) + (4 * T + T + 1), arrivals=n * (8 * T) + 16 * T)
                        if c or before:
                            transposed(n * NCH + c, (c + 1) % NCH)
                        act.wait_ge(s["shifted"], unit)
                        nc.scalar.activation(lg[c][:, :, :].rearrange("p j k -> p (j k)"),
                                             lg[c][:, :, :].rearrange("p j k -> p (j k)"), ACT.Exp).then_inc(s["exp"], 1)
                        nc.scalar.activation(tiny[:, 1, :], tiny[:, 1, :], ACT.Exp).then_inc(s["sinkexp"], 1)
                        act.wait_ge(w.projected, n * (NCH * T) + (2 * S + 4 + c * T + 2))
                        act.wait_ge(s["y"], unit)
                        nc.scalar.activation(sil[c][:, :], bank[1 + c][:, :], ACT.Tanh, scale=0.5, bias=cur[:, 1:2])\
                            .then_inc(s["tanh"], 1)
                        if c == 1 and not last:
                            w.round(act, 1, n * (NCH * T) + (4 * T + T + 2), arrivals=n * (8 * T) + 16 * T)
                act.sem_inc(s["y"], 2)
                body(0, False, False)
                with act.Fori(0, KT - 2) as i:
                    body(i + 1, False, True)
                body(KT - 1, True, True)
                transposed(KT * NCH, NCH - 1)

            @block.vector
            def _(dve):
                V = nc.vector
                b = core.col1[:, bias_at:bias_at + KT]
                bg = core.col1[:, bias_at + KT + 2:bias_at + 2 * KT + 2]
                V.tensor_scalar(par[:, :, 0], b, HD ** -0.5, None, op0=ALU.mult).then_inc(s["par"], 1)
                V.tensor_scalar(par[:, :, 1], bg, 0.5, None, op0=ALU.mult).then_inc(s["par"], 1)
                V.tensor_copy(par[:, :, 2], bg).then_inc(s["par"], 1)
                dve.wait_ge(s["vectors"], 32)
                by_pair = sink[:, :].rearrange("p (n b) -> p n b", b=2)
                for i in range(2):
                    rows = slice(i * QW, i * QW + QW)
                    V.tensor_copy(par[rows, :, 3], by_pair[rows, :, i]).then_inc(s["par"], 1)
                for i in range(KVH):
                    V.tensor_copy(kk[i][:, 0:QW], core.swa_keys[:, i, :]).then_inc(s["carried"], 1)
                V.tensor_copy(vals[:, 0, :], core.swa_values[:, 0, :]).then_inc(s["carried"], 1)
                for g in range(2):
                    dve.wait_ge(w.projected, 2 * S + 2 + g + 1)
                    V.tensor_tensor(vals[:, 1 + 4 * g:5 + 4 * g, :], bank[3 + g][:, :].rearrange("p (t k) -> p t k", t=4),
                                    bcast_mid(vbias[:, :], 4), ALU.add).then_inc(s["values"], 1)
                dve.wait_ge(s["par"], 5)
                dve.wait_ge(s["keys_doubled"], 32)
                dve.wait_ge(s["values"], 2)
                dve.wait_ge(s["carried"], 3)
                for i in range(KVH):
                    V.tensor_copy(core.swa_keys[:, i, :], kk[i][:, HALF:HALF + QW]).then_inc(s["carried"], 1)
                V.tensor_copy(core.swa_values[:, 0, :], vals[:, HALF // P, :]).then_inc(s["carried"], 1)
                V.tensor_copy(vals_even[0:QW, :, :], vals[0:QW, 1:, :]).then_inc(s["values"], 1)
                V.tensor_copy(vals_even[QW:P, :, :], vals[QW:P, 0:HALF // P, :]).then_inc(s["values"], 1)
                dve.wait_ge(s["bias"], 32)

                def out(unit, d, c):
                    dve.wait_ge(s["pv"], unit)
                    V.scalar_tensor_tensor(y[:, d, c * CH:c * CH + CH], bank[7][:, :], 0.5, sil[c][:, :],
                                           op0=ALU.mult, op1=ALU.mult).then_inc(s["y"], 1)

                def body(n, before, first):
                    V.tensor_copy(cur[:, :], par[:, n, :]).then_inc(s["cur"], 1)
                    dve.wait_ge(s["cur"], n + 1)
                    for c in range(NCH):
                        unit = n * NCH + (c + 1)
                        dve.wait_ge(s["qk"], unit)
                        for g in range(2):
                            src = bank[3 + g][:, :].rearrange("p (j w k) -> p j w k", j=2, w=2)
                            dst = lg[c][:, 4 * g:4 * g + 4, :].rearrange("p (j w) k -> p j w k", w=2)
                            for a in range(2):
                                there, here = slice(a * QW, a * QW + QW), slice((1 - a) * QW, (1 - a) * QW + QW)
                                V.tensor_tensor(dst[:, :, 0, there], src[:, :, 0, there],
                                                relb[:, n, here].unsqueeze(1).broadcast_to([P, 2, QW]), ALU.add)\
                                    .then_inc(s["logits"], 1)
                            V.tensor_tensor(dst[:, :, 1, :], src[:, :, 1, :],
                                            relb[:, n, :].unsqueeze(1).broadcast_to([P, 2, 2 * QW]), ALU.add)\
                                .then_inc(s["logits"], 1)
                        dve.wait_ge(s["logits"], n * (NCH * 6) + (6 * c + 6))
                        if half == 0 and c == 0:
                            V.memset(lg[0][:, 0, QW:2 * QW], MASKED).then_inc(s["masked"], 1)
                            dve.wait_ge(s["masked"], n + 1)
                        V.tensor_reduce(tiny[:, 0, :], lg[c][:, :, :], AX_X, ALU.max).then_inc(s["max"], 1)
                        dve.wait_ge(s["max"], n * (NCH * 2) + (2 * c + 1))
                        V.tensor_scalar(tiny[:, 0, :], tiny[:, 0, :], cur[:, 3:4], None, op0=ALU.max).then_inc(s["max"], 1)
                        dve.wait_ge(s["max"], n * (NCH * 2) + (2 * c + 2))
                        V.tensor_scalar(tiny[:, 1, :], tiny[:, 0, :], -1.0, cur[:, 3:4], op0=ALU.mult, op1=ALU.add)
                        V.tensor_tensor(lg[c][:, :, :], lg[c][:, :, :], bcast_last(tiny[:, 0, :], 2 * QW), ALU.subtract)\
                            .then_inc(s["shifted"], 1)
                        dve.wait_ge(s["exp"], unit)
                        V.tensor_reduce(tiny[:, 2, :], lg[c][:, :, :], AX_X, ALU.add).then_inc(s["den"], 1)
                        dve.wait_ge(s["den"], n * (NCH * 2) + (2 * c + 1))
                        dve.wait_ge(s["sinkexp"], unit)
                        V.tensor_tensor(tiny[:, 2, :], tiny[:, 2, :], tiny[:, 1, :], ALU.add).then_inc(s["den"], 1)
                        dve.wait_ge(s["den"], n * (NCH * 2) + (2 * c + 2))
                        if not (first and c == 0):
                            dve.wait_ge(s["probs"], n * NCH + c)
                        V.reciprocal(tiny[:, 3, :], tiny[:, 2, :]).then_inc(s["rec"], 1)
                        dve.wait_ge(s["tanh"], unit)
                        V.scalar_tensor_tensor(sil[c][:, :], bank[1 + c][:, :], cur[:, 2:3], sil[c][:, :],
                                               op0=ALU.add, op1=ALU.mult).then_inc(s["g1"], 1)
                        dve.wait_ge(s["g1"], unit)
                        V.scalar_tensor_tensor(sil[c][:, :], bank[1 + c][:, :], cur[:, 2:3], sil[c][:, :],
                                               op0=ALU.add, op1=ALU.add).then_inc(s["g2"], 1)
                        dve.wait_ge(s["g2"], unit)
                        if c:
                            out(n * NCH + c, n, 0)
                        elif before is not None:
                            out(n * NCH, before, NCH - 1)
                body(0, None, True)
                with dve.Fori(0, KT - 1) as i:
                    body(i + 1, i, False)
                out(KT * NCH, KT - 1, NCH - 1)


def hybrid_encoder(nc, A):
    depth = A["ada_w"].shape[0]
    seq = A["x"].shape[1]
    with ExitStack() as ctx:
        core = Core(nc, ctx)
        core.w_out = [A[n][0] for n in ("rg_w_out", "dn_w_out", "pool_w_out", "swa_w_out")[:depth]]
        core.carried = []
        if depth > 1:
            core.dn_halo = core.sb("dn_halo", [P, 3, H, 3])
            core.dn_state = core.sb("dn_state", [P, H, P])
            core.carried += [core.dn_halo, core.dn_state]
            core.dn_ab = core.sb("dn_ab", [P, P])
            core.dn_sums = core.sb("dn_sums", [P, P])
            core.dn_qkvz = nc.dram_tensor("dn_qkvz", (4, H, P, HALF), F32).ap()
        if depth > 2:
            core.pool_halo = core.sb("pool_halo", [P, KT, HALO])
            core.carried += [core.pool_halo]
        if depth > 3:
            core.swa_keys = core.sb("swa_keys", [P, KVH, QW])
            core.swa_values = core.sb("swa_values", [P, 1, KVH * HD])
            core.carried += [core.swa_keys, core.swa_values]
            core.swa_table = nc.dram_tensor("swa_table", (HQ, QW, REL), F32).ap()
        setup_phase(core, A, depth)
        core.x = core.sb("x_res", [P, KT, HALF])
        core.y = core.sb("y", [P, KT, HALF])
        core.open_h()
        for half in range(seq // HALF):
            residual_phase(core, A, half, -1, depth)
            for layer in range(depth):
                if layer == 0:
                    rg_phase(core, A, half)
                elif layer == 1:
                    dn_project_phase(core, A, half)
                    core.close_h()
                    dn_recur_phase(core, A, half)
                    core.open_h()
                elif layer == 2:
                    pool_phase(core, A, half)
                else:
                    swa_phase(core, A, half)
                residual_phase(core, A, half, layer, depth)
        core.close_h()


def delta_masks(np):
    r, c = np.arange(P)[:, None], np.arange(P)[None, :]
    parts = [r <= c]
    for s in LEVELS:
        parts.append((r // (2 * s) == c // (2 * s)) & (r % (2 * s) >= s) & (c % (2 * s) < s))
    cc = np.arange(32)[None, :]
    parts.append(r % 32 == cc)
    parts.append((r % 2 == 1) & (r % 32 - 1 == cc))
    return np.concatenate(parts, axis=1).astype(np.float32)


def pool_reciprocals(np):
    rows = [1.0 / np.minimum(np.arange(1, HALO + 1), win) for win in WINDOWS]
    return np.broadcast_to(np.stack(rows)[None], (P, NG, HALO)).astype(np.float32)


def relative_onehot(np):
    nb, max_exact = 16, 8
    rel = np.arange(REL) - 127
    n = np.abs(rel)
    large = max_exact + (np.log(np.maximum(n, 1) / max_exact) / np.log(128 / max_exact) * (nb - max_exact)).astype(np.int32)
    bucket = (rel > 0) * nb + np.where(n < max_exact, n, np.minimum(large, nb - 1))
    return (np.arange(2 * nb)[:, None] == bucket[None, :]).astype(np.float32)


_INS = ['x', 'c', 'ada_w', 'ada_b', 'norm_w', 'rel_bias', 'final_norm_w',
        'rg_w_in', 'rg_conv_w', 'rg_conv_b', 'rg_gate_w', 'rg_gate_b', 'rg_lambda', 'rg_w_out',
        'dn_w_in', 'dn_conv_w', 'dn_a_log', 'dn_dt_bias', 'dn_norm_w', 'dn_w_out',
        'pool_w_in', 'pool_group_w', 'pool_group_b', 'pool_scale', 'pool_w_out',
        'swa_w_in', 'swa_b_in', 'swa_sinks', 'swa_w_out']


def kernel(**inputs):
    import numpy as _np
    import concourse.bacc as _bacc
    from concourse import mybir as _mybir
    from concourse.bass_utils import run_bass_kernel_spmd as _run

    nc = _bacc.Bacc("TRN2", target_bir_lowering=False, num_devices=1)
    arrays, A = {}, {}
    for name in _INS:
        a = _np.ascontiguousarray(inputs[name])
        if a.size == 0:
            continue
        arrays[f"in_{name}"] = a
        A[name] = nc.dram_tensor(f"in_{name}", a.shape, _mybir.dt.from_np(a.dtype), kind="ExternalInput").ap()
    for name, a in (("delta_masks", delta_masks(_np)), ("pool_recip", pool_reciprocals(_np)),
                    ("rel_onehot", relative_onehot(_np))):
        arrays[name] = _np.ascontiguousarray(a)
        A[name] = nc.dram_tensor(name, a.shape, _mybir.dt.float32, kind="ExternalInput").ap()
    shape = tuple(inputs["x"].shape)
    A["out"] = nc.dram_tensor("out_0", shape, _mybir.dt.float32, kind="ExternalOutput").ap()
    hybrid_encoder(nc, A)
    r = _run(nc, [arrays], core_ids=[0])
    return r.results[0]["out_0"]
```
